# Optimizing a Trainium2 kernel written in Bass

```python
import jax, jax.numpy as jnp
from jax import lax
import numpy as np

D_MODEL = 2048
BATCH = 1
SEQ = 256
DEPTH = 2

CHUNK = 64
N_MIXERS = 2
POOL_WINDOWS = (2, 4, 8, 16)
N_POOL_GROUPS = len(POOL_WINDOWS)
POOL_GROUP_DIM = D_MODEL // N_POOL_GROUPS
HGRN_EXPAND = 128
HGRN_HEADS = D_MODEL // HGRN_EXPAND
HGRN_DK = HGRN_EXPAND
HGRN_DV = D_MODEL // HGRN_HEADS
D_FF = -(-8 * D_MODEL // (3 * 256)) * 256
N_MOD = 6
EPS = 1e-6

kernel_name = 'hybrid_pool_hgrn2_adaln_trunk'

def rms_norm(x, gain):
    xf = x.astype(jnp.float32)
    y = xf * lax.rsqrt(jnp.mean(xf * xf, axis=-1, keepdims=True) + EPS)
    return (y * gain.astype(jnp.float32)).astype(x.dtype)

def pool_mixer(h, w_group, chan_scale):
    B, S, D = h.shape
    hg = h.astype(jnp.float32).reshape(B, S, N_POOL_GROUPS, POOL_GROUP_DIM)
    cs = jnp.cumsum(hg, axis=1)
    pos = jnp.arange(1, S + 1, dtype=jnp.float32)
    outs = []
    for g, w in enumerate(POOL_WINDOWS):
        csg = cs[:, :, g]
        lo = jnp.concatenate([jnp.zeros((B, w, POOL_GROUP_DIM), jnp.float32), csg[:, :S - w]], axis=1)
        mean = (csg - lo) / jnp.minimum(pos, float(w))[None, :, None]
        outs.append(mean - hg[:, :, g])
    d = jnp.stack(outs, axis=2).astype(h.dtype)
    y = jnp.einsum('bsgc,gcd->bsgd', d, w_group).reshape(B, S, D)
    return y * chan_scale

def hgrn_lower_bounds(lb_params):
    p = jax.nn.softmax(lb_params.astype(jnp.float32), axis=0)
    return jnp.cumsum(p, axis=0) - p[0]

def hgrn2_mixer(h, w_in, w_out, out_norm_gain, lower_bound):
    B, S, D = h.shape
    nc = S // CHUNK
    proj = h @ w_in
    q, f_pre, v, g_out = jnp.split(proj, 4, axis=-1)
    f = lower_bound + (1.0 - lower_bound) * jax.nn.sigmoid(f_pre.astype(jnp.float32))
    log_f = jnp.log(f)
    k = 1.0 - f

    def to_chunks(t, dh):
        return t.astype(jnp.float32).reshape(B, nc, CHUNK, HGRN_HEADS, dh).transpose(1, 0, 3, 2, 4)

    qc = to_chunks(q, HGRN_DK)
    kc = to_chunks(k, HGRN_DK)
    vc = to_chunks(v, HGRN_DV)
    bc = jnp.cumsum(to_chunks(log_f, HGRN_DK), axis=3)
    mask = jnp.tril(jnp.ones((CHUNK, CHUNK), dtype=bool))

    def step(state, xs):
        q_c, k_c, v_c, b_c = xs
        diff = b_c[:, :, :, None, :] - b_c[:, :, None, :, :]
        decay = jnp.exp(jnp.where(mask[:, :, None], diff, -jnp.inf))
        scores = jnp.einsum('bhtd,bhsd,bhtsd->bhts', q_c, k_c, decay)
        o = (jnp.einsum('bhts,bhsv->bhtv', scores, v_c)
             + jnp.einsum('bhtd,bhdv->bhtv', q_c * jnp.exp(b_c), state))
        b_end = b_c[:, :, -1, :]
        state = (state * jnp.exp(b_end)[..., None]
                 + jnp.einsum('bhsd,bhsv->bhdv', k_c * jnp.exp(b_end[:, :, None, :] - b_c), v_c))
        return state, o

    state0 = jnp.zeros((B, HGRN_HEADS, HGRN_DK, HGRN_DV), jnp.float32)
    _, o = lax.scan(step, state0, (qc, kc, vc, bc))
    o = o.transpose(1, 0, 3, 2, 4).reshape(B, S, HGRN_HEADS, HGRN_DV)
    o = o * lax.rsqrt(jnp.mean(o * o, axis=-1, keepdims=True) + EPS)
    o = o.reshape(B, S, D) * out_norm_gain.astype(jnp.float32) * jax.nn.silu(g_out.astype(jnp.float32))
    return o.astype(h.dtype) @ w_out

def swiglu(h, w_in, w_out):
    a, b = jnp.split(h @ w_in, 2, axis=-1)
    return (jax.nn.silu(a) * b) @ w_out

def setup_inputs(seed: int = 0) -> dict:
    key = jax.random.key(seed)
    ks = jax.random.split(key, 16)
    n_pool = (DEPTH + 1) // 2
    n_hgrn = DEPTH // 2
    D, G = D_MODEL, POOL_GROUP_DIM
    nrm = jax.random.normal
    f32 = jnp.float32
    return {
        'x': nrm(ks[0], (BATCH, SEQ, D), f32),
        'c': nrm(ks[1], (BATCH, D), f32),
        'norm_mix_gain': 1.0 + 0.02 * nrm(ks[2], (DEPTH, D), f32),
        'norm_ffn_gain': 1.0 + 0.02 * nrm(ks[3], (DEPTH, D), f32),
        'w_ada': 0.5 * D ** -0.5 * nrm(ks[4], (DEPTH, D, N_MOD * D), f32),
        'b_ada': 0.02 * nrm(ks[5], (DEPTH, N_MOD * D), f32),
        'pool_w': G ** -0.5 * nrm(ks[6], (n_pool, N_POOL_GROUPS, G, G), f32),
        'pool_scale': 1.0 + 0.02 * nrm(ks[7], (n_pool, D), f32),
        'hgrn_w_in': D ** -0.5 * nrm(ks[8], (n_hgrn, D, 4 * D), f32),
        'hgrn_w_out': D ** -0.5 * nrm(ks[9], (n_hgrn, D, D), f32),
        'hgrn_norm_gain': 1.0 + 0.02 * nrm(ks[10], (n_hgrn, D), f32),
        'hgrn_lb': 1.0 + 0.1 * nrm(ks[11], (DEPTH, D), f32),
        'w_ffn_in': D ** -0.5 * nrm(ks[12], (DEPTH, D, 2 * D_FF), f32),
        'w_ffn_out': D_FF ** -0.5 * nrm(ks[13], (DEPTH, D_FF, D), f32),
        'final_gain': 1.0 + 0.02 * nrm(ks[14], (D,), f32),
    }

def reference(x, c, norm_mix_gain, norm_ffn_gain, w_ada, b_ada, pool_w, pool_scale,
              hgrn_w_in, hgrn_w_out, hgrn_norm_gain, hgrn_lb, w_ffn_in, w_ffn_out, final_gain):
    lower_bounds = hgrn_lower_bounds(hgrn_lb)
    cond = jax.nn.silu(c)
    for layer in range(DEPTH):
        mod = cond @ w_ada[layer] + b_ada[layer]
        sh_m, sc_m, g_m, sh_f, sc_f, g_f = jnp.split(mod[:, None, :], N_MOD, axis=-1)
        h = rms_norm(x, norm_mix_gain[layer]) * (1.0 + sc_m) + sh_m
        j = layer // N_MIXERS
        if layer % N_MIXERS == 0:
            y = pool_mixer(h, pool_w[j], pool_scale[j])
        else:
            y = hgrn2_mixer(h, hgrn_w_in[j], hgrn_w_out[j], hgrn_norm_gain[j],
                            lower_bounds[layer].astype(jnp.float32))
        x = x + g_m * y
        h = rms_norm(x, norm_ffn_gain[layer]) * (1.0 + sc_f) + sh_f
        x = x + g_f * swiglu(h, w_ffn_in[layer], w_ffn_out[layer])
    return rms_norm(x, final_gain)


_drawn_inputs = setup_inputs


def setup_inputs(seed=0):
    import zlib

    import numpy as np

    out = dict(_drawn_inputs(seed))
    spreads = {}
    factors = {'norm_mix_gain': 5.737,
     'norm_ffn_gain': 6.68,
     'pool_scale': 8.0,
     'hgrn_norm_gain': 8.0,
     'hgrn_lb': 3.54,
     'final_gain': 2.781}
    for name, (base, spread) in spreads.items():
        noise = np.random.default_rng([zlib.crc32(name.encode()), seed]).standard_normal(out[name].shape)
        drawn = base * np.exp(spread * noise) if base else spread * noise
        out[name] = __import__('jax').numpy.asarray(drawn.astype(out[name].dtype))
    for name, factor in factors.items():
        out[name] = (out[name] * factor).astype(out[name].dtype)
    return out
```

```python
from contextlib import ExitStack, contextmanager

import numpy as np
import concourse.bass as bass
from concourse import mybir

F32 = mybir.dt.float32
F32R = mybir.dt.float32r
BF16 = mybir.dt.bfloat16
ALU = mybir.AluOpType
ACT = mybir.ActivationFunctionType
AXX = mybir.AxisListType.X

P = 128
CH = 512
EPS = 1e-6
WINDOWS = (2, 4, 8, 16)
PAD = 16
LEVELS = (64, 32, 16, 8, 4, 2, 1)
LN_FLOOR = 2.0 ** -60


class Tally:

    def __init__(self):
        self.n = {}
        self.i = None
        self.first = 0
        self.per = {}

    def some(self, name, n=1):
        return self.get(name) >= n

    def get(self, name):
        return self.n.get(name, 0)

    def tick(self, name, k=1):
        self.n[name] = self.get(name) + k

    def value(self, name, add=0, scale=1, div=1):
        const = scale * (self.get(name) // div + add)
        if self.i is None or not self.per.get(name, 0):
            return const
        assert self.per[name] % div == 0
        step = scale * self.per[name] // div
        return self.i * step + (const - self.first * step)

    @contextmanager
    def loop(self, eng, count, per, first=0):
        before = dict(self.n)
        with eng.Fori(first, first + count) as i:
            self.i, self.first, self.per = i, first, per
            yield i
        for name in list(self.n):
            grown = self.get(name) - before.get(name, 0)
            assert grown in (0, per.get(name, 0)), (name, grown, per.get(name, 0))
            self.n[name] = before.get(name, 0) + count * grown
        self.i, self.per = None, {}


def due(step, n, first, last):
    return [k for k in range(n) if first + k * (last - first + 1) // n == step]


def build(nc, x, c, norm_mix_gain, norm_ffn_gain, w_ada, b_ada, pool_w, pool_scale, hgrn_w_in,
          hgrn_w_out, hgrn_norm_gain, hgrn_lb, w_ffn_in, w_ffn_out, final_gain, out):
    D = x.shape[2]
    TB = x.shape[1] // P
    S = TB * P
    KD = D // P
    NCH = D // CH
    F = w_ffn_out.shape[1]
    KF = F // P
    NF = F // CH
    HG = CH // P
    KU = KD // 2
    NL = 3 + len(LEVELS)
    RAW = 4
    SPL = 4
    ADA = 4

    EVAC = 3
    TURN = 6
    IN_UNIT = (0, 24)
    FIRST_UNITS = [(0, 12), (16, 28)]
    OUT_UNITS = {1: [(0, 31)], 2: [(0, 15), (20, 35)]}
    WOUT_UNIT = (3, 13)
    SUM = 2
    LEVEL_AT, LEVEL_EVERY = 8, 3

    def per(steps, chunks, units=0, **more):
        return dict(step=steps, raw=steps // 2, prod=chunks, unit=units, ada=KU * units, **more)

    PER_2UNITS = dict(unit=2, ada=2 * KU)
    PER_IN = per(2 * KD, 2, 0, small0=1, small1=1, hid=2)
    PER_IN_UNIT = per(2 * KD, 2, 1, small0=1, small1=1, hid=2)
    PER_OUT = {n: per(2 * KF, 2, 2 * n, upd=2, sq=2 * TB) for n in (1, 2)}
    PER_WOUT = per(2 * KD, 2, 2, upd=2, sq=2 * TB)
    PER_HGRN = per(4 * KD, 4, 0, small0=3 + NL // 2, small1=3 + NL // 2, level=NL - 2, group=1)

    CLOSE = 5 * NCH

    def unit_buffer(t):
        return t.get("unit") % 2 if t.get("unit") < CLOSE else 0

    def unit_lag(t):
        return 1 if t.get("unit") < CLOSE else 0

    ctx = ExitStack()
    with ctx:
        def sb(name, shape, dt=F32, where=ctx):
            return where.enter_context(nc.sbuf_tensor(name, shape, dt))

        def sem(name):
            return ctx.enter_context(nc.semaphore(name))

        xs = sb("xs", [P, TB, D])
        h_hi = sb("h_hi", [P, KD, S], F32R)
        h_lo = sb("h_lo", [P, KD, S], F32R)
        raw = sb("raw", [P, RAW, 2, CH])
        w_hi = sb("w_hi", [P, SPL, CH], F32R)
        w_lo = sb("w_lo", [P, SPL, CH], F32R)
        ada = sb("ada", [P, ADA, 2, CH])
        acc = sb("acc", [P, 2, CH])
        bias = sb("bias", [1, 2, CH])
        gate = sb("gate", [P, CH])
        tok = sb("tok", [P, TB, CH])
        feat = sb("feat", [P, 2, 2, S])
        junk = sb("junk", [P, CH], BF16)
        ident = sb("ident", [P, P])
        ones = sb("ones", [P, P])
        cols = sb("cols", [P, P])
        cond = sb("cond", [P, KD])
        mod = sb("mod", [P, 2, 2 * KD])
        gain = sb("gain", [P, KD])
        zero = sb("zero", [P, KD])
        lower = sb("lower", [P, KD])
        upper = sb("upper", [P, KD])
        ssq = sb("ssq", [P, TB, NCH])
        rstd = sb("rstd", [P, TB])

        with ExitStack() as pooling:
            rows = sb("rows", [P, P], where=pooling)
            pscale = sb("pscale", [P, CH], where=pooling)
            padded = sb("padded", [P, HG, PAD + S], where=pooling)
            win = [sb(f"win{i}", [P, HG, PAD + S], where=pooling) for i in range(2)]
            diff = sb("diff", [P, HG, S], where=pooling)
            edge = sb("edge", [P, HG, PAD], where=pooling)
            inv = sb("inv", [P, PAD], where=pooling)
            lbt = sb("lbt", [P, 4, KD], where=pooling)
        with ExitStack() as hgrn:
            keep = sb("keep", [P, HG * S], BF16, where=hgrn)
            masks = sb("masks", [P, len(LEVELS), P // 2], where=hgrn)
            fT = sb("fT", [P, HG, S], where=hgrn)
            kT = sb("kT", [P, HG, S], where=hgrn)
            bT = sb("bT", [P, HG, S], where=hgrn)
            qT = sb("qT", [P, HG, S], where=hgrn)
            dec = sb("dec", [P, 2, HG, S], where=hgrn)
            kdec = sb("kdec", [P, 2, HG, S], where=hgrn)
            qdec = sb("qdec", [P, 2, HG, P], where=hgrn)
            sdiag = sb("sdiag", [P, HG, TB, P], where=hgrn)
            scross = sb("scross", [P, HG, P], where=hgrn)
            smask = sb("smask", [P, HG * TB, P // 2], where=hgrn)
            vt = sb("vt", [P, TB, CH], where=hgrn)
            sg = sb("sg", [P, TB, CH], where=hgrn)
            hn = sb("hn", [P, TB, HG], where=hgrn)
            og = sb("og", [P, TB, D], where=hgrn)
            w_hi2 = sb("w_hi2", [P, SPL, CH], F32R, where=hgrn)
            w_lo2 = sb("w_lo2", [P, SPL, CH], F32R, where=hgrn)
        g_hi = sb("g_hi", [P, KF, S], F32R)
        g_lo = sb("g_lo", [P, KF, S], F32R)
        sq = fT[:, :, :].rearrange("p a s -> p (a s)").rearrange("p (t n) -> p t n", t=TB)
        fgain = ada[:, 0:2].rearrange("p a b n -> p (a b n)")

        prod = [ctx.enter_context(nc.psum_tensor(f"prod{i}", [P, TB, CH], F32)) for i in range(2)]
        small = [ctx.enter_context(nc.psum_tensor(f"small{i}", [P, CH], F32)) for i in range(2)]
        modp = ctx.enter_context(nc.psum_tensor("modp", [P, CH], F32))

        C_GMIX, C_GFFN, C_HGAIN, C_LB = KD, 3 * KD, 5 * KD, 6 * KD

        raw_loaded = [sem(f"raw_loaded{i}") for i in range(RAW)]
        ada_loaded = [sem(f"ada_loaded{i}") for i in range(ADA)]
        params_loaded = sem("params_loaded")
        x_loaded = sem("x_loaded")
        bias_loaded = [sem(f"bias_loaded{i}") for i in range(2)]
        pscale_loaded = sem("pscale_loaded")
        fgain_loaded = sem("fgain_loaded")
        stored = sem("stored")
        consts = sem("consts")
        hgrn_consts = sem("hgrn_consts")
        w_used = sem("w_used")
        unit_reduced = sem("unit_reduced")
        small_full = [sem(f"small_full{i}") for i in range(2)]
        hi_ready = sem("hi_ready")
        unit_taken = sem("unit_taken")
        cond_ready = sem("cond_ready")
        lb_exp = sem("lb_exp")
        squared = sem("squared")
        rstd_ready = sem("rstd_ready")
        ghi_ready = sem("ghi_ready")
        log_ready = sem("log_ready")
        dec_ready = sem("dec_ready")
        osq_ready = sem("osq_ready")
        orstd_ready = sem("orstd_ready")
        lo_ready = sem("lo_ready")
        ada_half = sem("ada_half")
        ada_used = sem("ada_used")
        unit_summed = sem("unit_summed")
        cols_ready = sem("cols_ready")
        lb_max = sem("lb_max")
        lb_ready = sem("lb_ready")
        var_step = sem("var_step")
        var_ready = sem("var_ready")
        tok_ready = sem("tok_ready")
        h_high = sem("h_high")
        h_ready = sem("h_ready")
        pool_step = sem("pool_step")
        pscale_ready = sem("pscale_ready")
        x_updated = sem("x_updated")
        f_ready = sem("f_ready")
        fT_ready = sem("fT_ready")
        b_ready = sem("b_ready")
        arg_ready = sem("arg_ready")
        qk_ready = sem("qk_ready")
        s_masked = sem("s_masked")
        s_ready = sem("s_ready")
        ovar_step = sem("ovar_step")
        ovar_ready = sem("ovar_ready")
        og_ready = sem("og_ready")
        final_step = sem("final_step")
        y_ready = sem("y_ready")
        prod_free = [sem(f"prod_free{i}") for i in range(2)]
        small_free = [sem(f"small_free{i}") for i in range(2)]

        def split_slot(t, deep):
            k = t.get("step") % (2 * SPL if deep else SPL)
            return (w_hi[:, k], w_lo[:, k]) if k < SPL else (w_hi2[:, k - SPL], w_lo2[:, k - SPL])

        block = ctx.enter_context(nc.Block())
        FFN_STEPS = 2 * KD * NF + KF * NCH

        @block.sync
        def _(sp):
            t = Tally()

            def load_w(src):
                slot = t.get("raw") % RAW
                if t.some("raw", RAW):
                    sp.wait_ge(lo_ready, t.value("raw", 1 - RAW, 2))
                sp.dma_start(raw[:, slot], src.rearrange("(a p) n -> p a n", p=P)).then_inc(raw_loaded[slot], 16)
                t.tick("raw")

            def load_ada(layer, at, k):
                if k == 0:
                    buf = unit_buffer(t)
                    if t.some("unit", 2):
                        sp.wait_ge(unit_summed, t.value("unit", -unit_lag(t)))
                    sp.dma_start(bias[:, buf], b_ada[layer:layer + 1, bass.ds(at, CH)]).then_inc(bias_loaded[buf], 16)
                slot = t.get("ada") % ADA
                if t.some("ada", ADA):
                    sp.wait_ge(ada_used, t.value("ada", 1 - ADA))
                src = w_ada[layer, 2 * k * P:2 * (k + 1) * P, bass.ds(at, CH)]
                sp.dma_start(ada[:, slot], src.rearrange("(a p) n -> p a n", p=P)).then_inc(ada_loaded[slot], 16)
                t.tick("ada")
                if k == KU - 1:
                    t.tick("unit")

            def load_unit(layer, at):
                for k in range(KU):
                    load_ada(layer, at, k)

            def load_chunk(src, at, blocks, units=(), shift=0):
                for s in range(blocks):
                    if s % 2 == 0:
                        load_w(src[s * P:(s + 2) * P, bass.ds(at, CH)])
                    for layer, col, span in units:
                        for k in due(s + shift, KU, *span):
                            load_ada(layer, col, k)

            at = 0
            for src in (c, norm_mix_gain, norm_ffn_gain, hgrn_norm_gain, hgrn_lb):
                n = src.shape[0] * KD
                sp.dma_start(rows[at:at + n, :], src.rearrange("l (k p) -> (l k) p", p=P)).then_inc(params_loaded, 16)
                at += n
            for tb in range(TB):
                sp.dma_start(xs[:, tb], x[0, tb * P:(tb + 1) * P, :]).then_inc(x_loaded, 16)
            load_unit(0, 0)
            load_unit(0, CH)
            with t.loop(sp, NCH - 1, PER_2UNITS) as i:
                load_unit(0, i * 2 * CH + 2 * CH)
                load_unit(0, i * 2 * CH + 3 * CH)
            for n in range(NCH):
                if n:
                    sp.wait_ge(x_updated, n)
                sp.dma_start(pscale[:, :], pool_scale[0:1, n * CH:(n + 1) * CH].to_broadcast([P, CH])).then_inc(pscale_loaded, 16)
                load_unit(0, 2 * D + n * CH)
                load_chunk(pool_w[0, n], 0, HG)
            with t.loop(sp, NCH, PER_2UNITS) as i:
                load_unit(0, i * 2 * CH + 3 * D)
                load_unit(0, i * 2 * CH + (3 * D + CH))

            def load_pair(at, units):
                load_chunk(w_ffn_in[0 if units is not None else 1], at, KD, units or ())
                load_chunk(w_ffn_in[0 if units is not None else 1], at + F, KD, units or (), KD)

            def load_ffn_out(layer):
                with t.loop(sp, NCH // 2, PER_OUT[2 - layer]) as i:
                    for o in range(2):
                        units = [(layer, i * 2 * CH + (5 * D + o * CH)), (1, i * 2 * CH + (3 * D + o * CH))]
                        load_chunk(w_ffn_out[layer], i * 2 * CH + o * CH, KF,
                                   [(*unit, span) for unit, span in zip(units, OUT_UNITS[2 - layer])])

            load_pair(0, [(1, 0, FIRST_UNITS[0]), (1, 4 * D, FIRST_UNITS[1])])
            with t.loop(sp, 2 * NCH - 1, PER_IN_UNIT) as i:
                load_pair(i * CH + CH, [(1, i * CH + CH, IN_UNIT)])
            with t.loop(sp, NF - 2 * NCH, PER_IN_UNIT) as i:
                load_pair(i * CH + 2 * NCH * CH, [(1, i * CH + (4 * D + CH), IN_UNIT)])
            load_ffn_out(0)
            with t.loop(sp, NCH, PER_HGRN, first=1) as i:
                for part in (1, 0, 2, 3):
                    load_chunk(hgrn_w_in[0], i * CH + (part * D - CH), KD)
            with t.loop(sp, NCH // 2, PER_WOUT) as i:
                for o in range(2):
                    load_chunk(hgrn_w_out[0], i * 2 * CH + o * CH, KD,
                               [(1, i * 2 * CH + (2 * D + o * CH), WOUT_UNIT)])
            with t.loop(sp, NF, PER_IN) as i:
                load_pair(i * CH, None)
            load_ffn_out(1)
            sp.wait_ge(ada_used, t.value("ada"))
            sp.dma_start(fgain, final_gain.rearrange("(a n) -> a n", a=1).to_broadcast([P, D])).then_inc(fgain_loaded, 16)
            for tb in range(TB):
                sp.wait_ge(y_ready, tb + 1)
                sp.dma_start(out[0, tb * P:(tb + 1) * P, :], xs[:, tb]).then_inc(stored, 16)
            sp.wait_ge(stored, 16 * TB)

        N_CONSTS = 4 + PAD + 1
        N_HGRN_CONSTS = 4 + 2 * len(LEVELS)

        @block.gpsimd
        def _(pool):
            pool.memset(ident[:, :], 0.0).then_inc(consts, 1)
            pool.memset(ones[:, :], 1.0).then_inc(consts, 1)
            pool.memset(zero[:, :], 0.0).then_inc(consts, 1)
            pool.memset(padded[:, :, 0:PAD], 0.0).then_inc(consts, 1)
            for n in range(PAD):
                pool.memset(inv[:, n:n + 1], 1.0 / (n + 1)).then_inc(consts, 1)
            pool.wait_ge(consts, 4 + PAD)
            pool.affine_select(out=ident[:, :], in_=ident[:, :], compare_op=ALU.not_equal, fill=1.0,
                               base=0, pattern=[[-1, P]], channel_multiplier=1).then_inc(consts, 1)
            pool.wait_ge(w_used, HG * NCH + FFN_STEPS)
            pool.memset(keep[:, :], 1.0).then_inc(hgrn_consts, 1)
            pool.memset(masks[:, :, :], 1.0).then_inc(hgrn_consts, 1)
            pool.memset(kdec[:, :, :, :], 0.0).then_inc(hgrn_consts, 1)
            pool.wait_ge(hgrn_consts, 3)
            pool.memset(keep[:, :].rearrange("p (n c) -> p n c", c=P)[:, :, 0:1], 0.0).then_inc(hgrn_consts, 1)
            for j, h in enumerate(LEVELS):
                m = masks[:, j, :].rearrange("p (b o) -> p b o", o=h)
                pool.affine_select(out=m, in_=m, compare_op=ALU.is_ge, fill=0.0, base=0,
                                   pattern=[[-2 * h, P // (2 * h)], [0, h]], channel_multiplier=1).then_inc(hgrn_consts, 1)
            pool.wait_ge(hgrn_consts, 4 + len(LEVELS))
            for j, h in enumerate(LEVELS):
                m = masks[:, j, :].rearrange("p (b o) -> p b o", o=h)
                pool.affine_select(out=m, in_=m, compare_op=ALU.is_ge, fill=0.0, base=h - 1,
                                   pattern=[[2 * h, P // (2 * h)], [0, h]], channel_multiplier=-1).then_inc(hgrn_consts, 1)

        @block.tensor
        def _(pe):
            t = Tally()

            def bank(n):
                if t.some(f"small{n}"):
                    pe.wait_ge(small_free[n], t.value(f"small{n}"))

            def filled(ins, n):
                ins.then_inc(small_full[n], 1)
                t.tick(f"small{n}")

            def product(hi, lo, blocks, after=None, deep=False):
                par = t.get("prod") % 2
                if t.some("prod", 2):
                    pe.wait_ge(prod_free[par], t.value("prod", 0, 1, 2))
                for k in range(blocks):
                    wh, wl = split_slot(t, deep)
                    pe.wait_ge(lo_ready, t.value("step", 1))
                    for tb in range(TB):
                        ts = slice(tb * P, (tb + 1) * P)
                        o = prod[par][:, tb]
                        pe.matmul(o, hi(k)[:, ts], wh, start=(k == 0), stop=False)
                        pe.matmul(o, hi(k)[:, ts], wl, start=False, stop=False)
                        mm = pe.matmul(o, lo(k)[:, ts], wh, start=False, stop=(k == blocks - 1))
                    mm.then_inc(w_used, 1)
                    t.tick("step")
                    if after is not None:
                        after(k)
                t.tick("prod")

            def h_product(after=None, deep=False):
                product(lambda k: h_hi[:, k], lambda k: h_lo[:, k], KD, after, deep)

            def reduce_unit(rowwise):
                a = acc[:, unit_buffer(t)]
                pe.wait_ge(unit_summed, t.value("unit", 1))
                if t.some("unit"):
                    pe.wait_ge(unit_taken, t.value("unit"))
                if rowwise:
                    mm = pe.matmul(modp[:, :], ones[:, :], a, start=True, stop=True)
                else:
                    for j in range(HG):
                        mm = pe.matmul(modp[:, j:j + 1], a[:, j * P:(j + 1) * P], ones[:, 0:1], start=True, stop=True)
                mm.then_inc(unit_reduced, 1)
                t.tick("unit")

            def turn(block_of):
                for half in range(2):
                    bank(half)
                    for j in range(2):
                        for tb in range(TB):
                            o = (j * TB + tb) * P
                            mm = pe.transpose(small[half][:, o:o + P], block_of(tb, 2 * half + j), ident[:, :])
                    filled(mm, half)

            def turn_tok():
                turn(lambda tb, b: tok[:, tb, b * P:(b + 1) * P])

            def turn_normalised():
                t.tick("tok")
                pe.wait_ge(tok_ready, t.value("tok"))
                turn_tok()

            def features():
                for n in range(NCH):
                    turn_normalised()
                t.tick("h", 2 * NCH)
                pe.wait_ge(h_ready, t.value("h"))

            pe.wait_ge(consts, N_CONSTS)
            pe.wait_ge(params_loaded, 16 * 5)
            filled(pe.transpose(small[0][:, 0:P], rows[:, :], ident[:, :]), 0)
            reduce_unit(False)
            reduce_unit(False)
            with t.loop(pe, NCH - 1, PER_2UNITS):
                reduce_unit(False)
                reduce_unit(False)
            for n in range(NCH):
                turn_normalised()
                reduce_unit(True)
                t.tick("h", 2)
                pe.wait_ge(h_ready, t.value("h"))
                product(lambda k: h_hi[:, n * HG + k], lambda k: h_lo[:, n * HG + k], HG)
            with t.loop(pe, NCH, PER_2UNITS):
                reduce_unit(False)
                reduce_unit(False)

            def turn_hidden():
                pe.wait_ge(prod_free[1], t.value("prod", 0, 1, 2))
                turn_tok()

            def ffn_pair(first, units):
                def in_gate(k):
                    if k == TURN and not first:
                        turn_hidden()
                    if k in [last + SUM for _, last in units]:
                        reduce_unit(False)

                def in_value(k):
                    if k + KD in [last + SUM for _, last in units]:
                        reduce_unit(False)

                h_product(in_gate)
                h_product(in_value)

            def ffn_out(layer):
                pe.wait_ge(small_free[0], t.value("small0"))
                pe.wait_ge(small_free[1], t.value("small1"))
                spans = OUT_UNITS[2 - layer]

                def in_out(k):
                    if k == spans[0][1] + SUM:
                        reduce_unit(True)
                    if layer == 0 and k == spans[1][1] + SUM:
                        reduce_unit(False)

                with t.loop(pe, NCH // 2, PER_OUT[2 - layer]):
                    for o in range(2):
                        product(lambda k: g_hi[:, k], lambda k: g_lo[:, k], KF, in_out)

            features()
            ffn_pair(True, FIRST_UNITS)
            with t.loop(pe, NF - 1, PER_IN_UNIT):
                ffn_pair(False, [IN_UNIT])
            turn_hidden()
            ffn_out(0)

            features()

            def self_scores(k):
                bank(k)
                pe.wait_ge(b_ready, t.value("group", 1))
                if k == 0:
                    pe.wait_ge(small_free[1], t.value("small1"))
                for hd in (2 * k, 2 * k + 1):
                    for blk in range(TB):
                        o = ((hd % 2) * TB + blk) * P
                        ts = slice(blk * P, (blk + 1) * P)
                        mm = pe.matmul(small[k][:, o:o + P], kT[:, hd, ts], qT[:, hd, ts], start=True, stop=True)
                filled(mm, k)

            def level_scores(j):
                b, H = j % 2, P // 2
                bank(b)
                t.tick("level")
                pe.wait_ge(qk_ready, t.value("level"))
                for hd in range(HG):
                    if j == 0:
                        mm = pe.matmul(small[b][:, hd * P:(hd + 1) * P], kdec[:, b, hd, 0:P], qdec[:, b, hd, :],
                                       start=True, stop=True)
                        continue
                    for blk in range(TB):
                        o = (hd * TB + blk) * H
                        mm = pe.matmul(small[b][:, o:o + H], kdec[:, b, hd, blk * P:(blk + 1) * P],
                                       qdec[:, b, hd, blk * H:(blk + 1) * H], start=True, stop=True)
                filled(mm, b)

            def in_q(k):
                if k == TURN:
                    pe.wait_ge(prod_free[0], t.value("prod", 1, 1, 2))
                    turn_tok()

            def in_v(k):
                if k == TURN:
                    pe.wait_ge(prod_free[1], t.value("prod", 0, 1, 2))
                    turn_tok()
                if k in (TURN + 2, TURN + 3):
                    self_scores(k - TURN - 2)
                for j in range(NL - 2):
                    if k == LEVEL_AT + LEVEL_EVERY * j + 2:
                        level_scores(j)

            def in_g(k):
                for j in range(NL - 2):
                    if k + KD == min(LEVEL_AT + LEVEL_EVERY * j + 2, 2 * KD - 1):
                        level_scores(j)

            with t.loop(pe, NCH, PER_HGRN):
                h_product(None, True)
                h_product(in_q, True)
                h_product(in_v, True)
                h_product(in_g, True)
                t.tick("group")
                pe.wait_ge(s_ready, t.value("group"))
                pe.wait_ge(prod_free[0], t.value("prod", 0, 1, 2))
                for tb in range(TB):
                    bank(tb)
                    for hd in range(HG):
                        hs = slice(hd * P, (hd + 1) * P)
                        if tb:
                            pe.matmul(small[tb][:, hs], scross[:, hd], vt[:, 0, hs], start=True, stop=False)
                        mm = pe.matmul(small[tb][:, hs], sdiag[:, hd, tb], vt[:, tb, hs], start=(tb == 0), stop=True)
                    filled(mm, tb)
            pe.wait_ge(og_ready, NCH)
            for n in range(NCH):
                turn(lambda tb, b: og[:, tb, (n * HG + b) * P:(n * HG + b + 1) * P])
            t.tick("h", 2 * NCH)
            pe.wait_ge(h_ready, t.value("h"))
            with t.loop(pe, NCH // 2, PER_WOUT):
                for o in range(2):
                    h_product()
                    reduce_unit(True)
            features()
            ffn_pair(True, [])
            with t.loop(pe, NF - 1, PER_IN):
                ffn_pair(False, [])
            turn_hidden()
            ffn_out(1)

        @block.scalar
        def _(act):
            t = Tally()

            def hi(deep=False):
                r = t.get("step") // 2 % RAW
                if t.get("step") % 2 == 0:
                    act.wait_ge(raw_loaded[r], t.value("step", 1, 16, 2 * RAW))
                if t.some("step", SPL):
                    act.wait_ge(w_used, t.value("step", 1 - (2 * SPL if deep else SPL)))
                act.activation(split_slot(t, deep)[0], raw[:, r, t.get("step") % 2], ACT.Copy).then_inc(hi_ready, 1)
                t.tick("step")

            def chunk(n, before=None, deep=False):
                for k in range(n):
                    if before is not None:
                        before(k)
                    hi(deep)
                t.tick("used", n)

            def take_columns(dst):
                act.wait_ge(unit_reduced, t.value("unit", 1))
                act.activation(dst, modp[:, 0:HG], ACT.Copy).then_inc(unit_taken, 1)
                t.tick("unit")

            def take_gate():
                act.wait_ge(unit_reduced, t.value("unit", 1))
                if t.some("upd"):
                    act.wait_ge(x_updated, t.value("upd"))
                act.activation(gate[:, :], modp[:, :], ACT.Copy).then_inc(unit_taken, 1)
                t.tick("unit")

            def square(at):
                for tb in range(TB):
                    if t.some("sq"):
                        act.wait_ge(squared, t.value("sq"))
                    act.activation(junk[:, :], xs[:, tb, bass.ds(at * CH, CH)], ACT.Square,
                                   accum_out=ssq[:, tb, bass.ds(at, 1)]).then_inc(squared, 1)
                    t.tick("sq")

            def square_updated(at):
                t.tick("upd")
                act.wait_ge(x_updated, t.value("upd"))
                square(at)

            def root():
                t.tick("norm")
                act.wait_ge(var_ready, t.value("norm"))
                act.activation(rstd[:, :], rstd[:, :], ACT.Sqrt).then_inc(rstd_ready, 1)

            def filled(half):
                t.tick(f"small{half}")
                act.wait_ge(small_full[half], t.value(f"small{half}"))

            def modulate(gains, shifts, n, into=None):
                for half in range(2):
                    filled(half)
                    if into is None:
                        act.wait_ge(h_ready, t.value("h", -1))
                    for j in range(2):
                        k = n * HG + 2 * half + j
                        dst = feat[:, half, j] if into is None else into[:, 2 * half + j, PAD:]
                        ins = act.activation(dst, small[half][:, j * S:(j + 1) * S], ACT.Identity,
                                             bias=shifts[:, k:k + 1], scale=gains[:, k:k + 1])
                    ins.then_inc(small_free[half], 1)
                    t.tick("h")

            def features(gains, shifts):
                for n in range(NCH):
                    modulate(gains, shifts, n)

            def take(par, dst, func):
                act.wait_ge(w_used, t.value("used"))
                act.activation(dst[:, :, :], prod[par][:, :, :], func).then_inc(prod_free[par], 1)

            act.wait_ge(cols_ready, 1)
            act.activation(cond[:, :], cols[:, 0:KD], ACT.Silu).then_inc(cond_ready, 1)
            act.wait_ge(x_loaded, 16 * TB)
            for n in range(NCH):
                square(n)
            act.wait_ge(lb_max, 3)
            act.activation(lbt[:, 2:4], lbt[:, 2:4], ACT.Exp).then_inc(lb_exp, 1)
            t.tick("small0")
            take_columns(mod[:, 0, 0:HG])
            take_columns(mod[:, 0, HG:2 * HG])
            with t.loop(act, NCH - 1, PER_2UNITS) as i:
                take_columns(mod[:, 0, bass.ds(i * 2 * HG + 2 * HG, HG)])
                take_columns(mod[:, 0, bass.ds(i * 2 * HG + 3 * HG, HG)])
            root()
            act.wait_ge(consts, N_CONSTS)
            for n in range(NCH):
                if n:
                    act.wait_ge(h_ready, 2 * n)
                modulate(gain, mod[:, 0, 0:KD], n, padded)
                take_gate()
                chunk(HG)
                square_updated(n)
            with t.loop(act, NCH, PER_2UNITS) as i:
                take_columns(mod[:, 1, bass.ds(i * 2 * HG, HG)])
                take_columns(mod[:, 1, bass.ds(i * 2 * HG + HG, HG)])

            def take_hidden(at, half):
                filled(half)
                act.activation(g_hi[:, bass.ds(at + 2 * half, 2), :],
                               small[half][:, :].rearrange("p (a s) -> p a s", a=2), ACT.Copy).then_inc(ghi_ready, 1)

            def ffn_pair(at, first, units):
                def in_gate(k):
                    if k == TURN + 3 and not first:
                        take_hidden(at, 0)
                    if k == TURN + 4 and not first:
                        take_hidden(at, 1)

                def in_value(k):
                    if k == 3 and len(units) == 2:
                        take_columns(units[0])
                    if k == EVAC:
                        take(0, tok, ACT.Silu)

                chunk(KD, in_gate)
                chunk(KD, in_value)
                if units:
                    take_columns(units[-1])

            def ffn_out(layer):
                spans = OUT_UNITS[2 - layer]
                with t.loop(act, NCH // 2, dict(PER_OUT[2 - layer], used=2 * KF)) as i:
                    for o in range(2):
                        def in_out(k):
                            if k == EVAC + 3 and o == 1:
                                square_updated(i * 2)
                            if k == spans[0][1] + SUM + 4:
                                take_gate()
                            if layer == 0 and k == spans[1][1] + SUM + 4:
                                take_columns(mod[:, 1, bass.ds(i * 2 * HG + o * HG, HG)])
                        chunk(KF, in_out)
                    square_updated(i * 2 + 1)

            root()
            features(gain, mod[:, 1, 0:KD])
            ffn_pair(0, True, [mod[:, 0, 0:HG], mod[:, 1, KD:KD + HG]])
            with t.loop(act, 2 * NCH - 1, dict(PER_IN_UNIT, used=2 * KD)) as i:
                ffn_pair(i * HG, False, [mod[:, 0, bass.ds(i * HG + HG, HG)]])
            with t.loop(act, NF - 2 * NCH, dict(PER_IN_UNIT, used=2 * KD)) as i:
                ffn_pair(i * HG + (2 * NCH - 1) * HG, False, [mod[:, 1, bass.ds(i * HG + (KD + HG), HG)]])
            take_hidden((NF - 1) * HG, 0)
            take_hidden((NF - 1) * HG, 1)
            ffn_out(0)

            root()
            features(gain, mod[:, 0, 0:KD])

            def features_of(dst, func):
                for half in range(2):
                    filled(half)
                    act.activation(dst[:, 2 * half:2 * half + 2, :],
                                   small[half][:, :].rearrange("p (a s) -> p a s", a=2), func).then_inc(small_free[half], 1)

            def decay(j):
                t.tick("level")
                act.wait_ge(arg_ready, t.value("level"))
                act.activation(dec[:, j % 2], dec[:, j % 2], ACT.Exp).then_inc(dec_ready, 1)

            def in_q(k):
                if k == EVAC:
                    take(0, tok, ACT.Copy)
                if k == TURN + 3:
                    features_of(fT, ACT.Sigmoid)
                if k == TURN + 6:
                    act.wait_ge(f_ready, t.value("group", 1))
                    act.activation(dec[:, 1], dec[:, 0], ACT.Ln).then_inc(log_ready, 1)

            def in_v(k):
                if k == EVAC:
                    take(1, tok, ACT.Copy)
                if k == TURN + 2:
                    features_of(qT, ACT.Copy)
                for j in range(NL - 2):
                    if k == LEVEL_AT + LEVEL_EVERY * j + 1:
                        decay(j)

            def in_g(k):
                if k == EVAC:
                    take(0, vt, ACT.Copy)
                for j in range(NL - 2):
                    if k + KD == LEVEL_AT + LEVEL_EVERY * j + 1:
                        decay(j)

            with t.loop(act, NCH, dict(PER_HGRN, used=4 * KD)) as i:
                chunk(KD, None, True)
                chunk(KD, in_q, True)
                chunk(KD, in_v, True)
                chunk(KD, in_g, True)
                take(1, sg, ACT.Silu)
                t.tick("small0", NL // 2)
                t.tick("small1", NL // 2)
                for tb in range(TB):
                    filled(tb)
                    act.activation(sq[:, tb], small[tb][:, :], ACT.Square).then_inc(osq_ready, 1)
                t.tick("group")
                act.wait_ge(ovar_ready, t.value("group"))
                act.activation(hn[:, :, :], hn[:, :, :], ACT.Sqrt).then_inc(orstd_ready, 1)
            features(cols[:, C_HGAIN:C_HGAIN + KD], zero)
            with t.loop(act, NCH // 2, dict(PER_WOUT, used=2 * KD)) as i:
                def in_second(k):
                    if k == EVAC:
                        take_gate()
                    if k == EVAC + 4:
                        square_updated(i * 2)
                chunk(KD)
                chunk(KD, in_second)
                take_gate()
                square_updated(i * 2 + 1)
            root()
            features(gain, mod[:, 1, 0:KD])
            ffn_pair(0, True, [])
            with t.loop(act, NF - 1, dict(PER_IN, used=2 * KD)) as i:
                ffn_pair(i * HG, False, [])
            take_hidden((NF - 1) * HG, 0)
            take_hidden((NF - 1) * HG, 1)
            ffn_out(1)
            root()

        @block.vector
        def _(dve):
            t = Tally()

            def lo(deep=False):
                r = t.get("step") // 2 % RAW
                wh, wl = split_slot(t, deep)
                dve.wait_ge(hi_ready, t.value("step", 1))
                dve.tensor_tensor(wl, raw[:, r, t.get("step") % 2], wh, ALU.subtract).then_inc(lo_ready, 1)
                t.tick("step")

            def chunk(n, after=None, deep=False):
                for k in range(n):
                    lo(deep)
                    if after is not None:
                        after(k)
                t.tick("used", n)

            def fold(k):
                slot, buf = t.get("ada") % ADA, unit_buffer(t)
                w, a = ada[:, slot, k % 2], acc[:, buf]
                if k == 0:
                    dve.wait_ge(ada_loaded[slot], t.value("ada", 1, 16, ADA))
                    if t.some("unit", 2):
                        dve.wait_ge(unit_reduced, t.value("unit", -unit_lag(t)))
                    dve.tensor_scalar(a, w, cond[:, 0:1], None, ALU.mult).then_inc(ada_half, 1)
                elif k % 2 == 0:
                    dve.wait_ge(ada_loaded[slot], t.value("ada", 1, 16, ADA))
                    dve.wait_ge(ada_used, t.value("ada"))
                    dve.scalar_tensor_tensor(a, w, cond[:, k:k + 1], a, ALU.mult, ALU.add).then_inc(ada_half, 1)
                else:
                    dve.wait_ge(ada_half, t.value("ada", 1))
                    dve.scalar_tensor_tensor(a, w, cond[:, k:k + 1], a, ALU.mult, ALU.add).then_inc(ada_used, 1)
                    t.tick("ada")
                if k == KD - 1:
                    dve.wait_ge(ada_used, t.value("ada"))
                    if t.get("unit") < CLOSE:
                        dve.wait_ge(bias_loaded[buf], t.value("unit", 1, 16, 2))
                    else:
                        dve.wait_ge(bias_loaded[0], t.value("unit", 1 - CLOSE // 2, 16))
                    dve.tensor_tensor(a[0:1, :], a[0:1, :], bias[:, buf], ALU.add).then_inc(unit_summed, 1)
                    t.tick("unit")

            def unit():
                for k in range(KD):
                    fold(k)

            def norm_prepare(gains, branch):
                if gains is not None:
                    dve.wait_ge(unit_taken, t.value("unit"))
                    dve.scalar_tensor_tensor(gain[:, :], mod[:, branch, KD:2 * KD], 1.0, cols[:, gains:gains + KD],
                                             ALU.add, ALU.mult)
                dve.wait_ge(squared, t.value("sq"))
                dve.tensor_reduce(rstd[:, :], ssq[:, :, :], AXX, ALU.add).then_inc(var_step, 1)
                t.tick("var")
                dve.wait_ge(var_step, t.value("var"))
                dve.tensor_scalar(rstd[:, :], rstd[:, :], 1.0 / D, EPS, ALU.mult, ALU.add).then_inc(var_step, 1)
                t.tick("var")
                dve.wait_ge(var_step, t.value("var"))
                dve.reciprocal(rstd[:, :], rstd[:, :]).then_inc(var_ready, 1)
                t.tick("norm")
                dve.wait_ge(rstd_ready, t.value("norm"))

            def normalise(n):
                if t.some("small1"):
                    dve.wait_ge(small_full[1], t.value("small1"))
                if t.some("upd"):
                    dve.wait_ge(x_updated, t.value("upd"))
                for tb in range(TB):
                    ins = dve.tensor_scalar(tok[:, tb], xs[:, tb, n * CH:(n + 1) * CH], rstd[:, tb:tb + 1], None, ALU.mult)
                ins.then_inc(tok_ready, 1)

            def split_h(src, k, n):
                dve.tensor_copy(h_hi[:, k:k + n], src).then_inc(h_high, 1)
                t.tick("hh")
                dve.wait_ge(h_high, t.value("hh"))
                return dve.tensor_tensor(h_lo[:, k:k + n], src, h_hi[:, k:k + n], ALU.subtract)

            def split_feat(n):
                for half in range(2):
                    t.tick(f"small{half}")
                    dve.wait_ge(small_free[half], t.value(f"small{half}"))
                    split_h(feat[:, half], n * HG + 2 * half, 2).then_inc(h_ready, 1)

            def features(gains, branch):
                norm_prepare(gains, branch)
                normalise(0)
                for n in range(NCH):
                    if n + 1 < NCH:
                        t.n["small1"] += 1
                        normalise(n + 1)
                        t.n["small1"] -= 1
                    split_feat(n)

            def update(par, at, gates=gate, later=0):
                dve.wait_ge(w_used, t.value("used"))
                dve.wait_ge(unit_taken, t.value("unit", -later))
                if t.some("upd"):
                    dve.wait_ge(x_updated, t.value("upd"))
                t.tick("upd")
                term = gates[:, :].unsqueeze(1).to_broadcast([P, TB, CH])
                dve.tensor_tensor(tok[:, :, :], prod[par][:, :, :], term, ALU.mult).then_inc(prod_free[par], 1)
                dve.wait_ge(prod_free[par], t.value("prod", 1, 1, 2))
                xc = xs[:, :, bass.ds(at * CH, CH)]
                dve.tensor_tensor(xc, xc, tok[:, :, :], ALU.add).then_inc(x_updated, 1)

            dve.wait_ge(small_full[0], 1)
            dve.tensor_copy(cols[:, :], small[0][:, 0:P]).then_inc(small_free[0], 1)
            t.tick("small0")
            dve.wait_ge(small_free[0], 1)
            lb = cols[:, C_LB:C_LB + 2 * KD].rearrange("p (l k) -> p l k", l=2)
            dve.tensor_copy(lbt[:, 2:4], lb).then_inc(cols_ready, 1)
            dve.tensor_tensor(lbt[:, 0], lb[:, 0], lb[:, 1], ALU.max).then_inc(lb_max, 1)
            dve.wait_ge(lb_max, 1)
            dve.wait_ge(cols_ready, 1)
            for l in range(2):
                dve.tensor_tensor(lbt[:, 2 + l], lbt[:, 2 + l], lbt[:, 0], ALU.subtract).then_inc(lb_max, 1)
            dve.wait_ge(lb_exp, 1)
            dve.tensor_tensor(lbt[:, 0], lbt[:, 2], lbt[:, 3], ALU.add).then_inc(lb_ready, 1)
            dve.wait_ge(lb_ready, 1)
            dve.reciprocal(lbt[:, 1], lbt[:, 0]).then_inc(lb_ready, 1)
            dve.wait_ge(lb_ready, 2)
            for l in range(2):
                dve.tensor_tensor(lbt[:, 2 + l], lbt[:, 2 + l], lbt[:, 1], ALU.mult).then_inc(lb_ready, 1)
            dve.wait_ge(lb_ready, 4)
            dve.tensor_tensor(lbt[:, 0], lbt[:, 2], lbt[:, 3], ALU.add).then_inc(lb_ready, 1)
            dve.wait_ge(lb_ready, 5)
            dve.tensor_tensor(lower[:, :], lbt[:, 0], lbt[:, 2], ALU.subtract).then_inc(lb_ready, 1)
            dve.wait_ge(lb_ready, 6)
            dve.tensor_scalar(upper[:, :], lower[:, :], -1.0, 1.0, ALU.mult, ALU.add).then_inc(lb_ready, 1)
            dve.wait_ge(cond_ready, 1)
            t.tick("sq", NCH * TB)
            unit()
            unit()
            with t.loop(dve, NCH - 1, PER_2UNITS):
                unit()
                unit()

            def pool_group(n, w):
                src, span, lo_end = padded, 1, 1
                step = [t.get("pool")]

                def done(ins):
                    ins.then_inc(pool_step, 1)
                    t.tick("pool")
                    dve.wait_ge(pool_step, t.value("pool"))

                while span < w:
                    dst = win[0] if src is not win[0] else win[1]
                    done(dve.tensor_tensor(dst[:, :, lo_end:], src[:, :, lo_end:],
                                           src[:, :, lo_end - span:PAD + S - span], ALU.add))
                    src, span = dst, 2 * span
                    lo_end += span
                h = padded[:, :, PAD:]
                done(dve.scalar_tensor_tensor(diff[:, :, :], src[:, :, PAD:], 1.0 / w, h, ALU.mult, ALU.subtract))
                done(dve.tensor_tensor(edge[:, :, 0:w], src[:, :, PAD:PAD + w],
                                       inv[:, 0:w].unsqueeze(1).to_broadcast([P, HG, w]), ALU.mult))
                done(dve.tensor_tensor(diff[:, :, 0:w], edge[:, :, 0:w], h[:, :, 0:w], ALU.subtract))
                split_h(diff[:, :, :], n * HG, HG).then_inc(h_ready, 2)

            norm_prepare(C_GMIX, 0)
            for n, w in enumerate(WINDOWS):
                normalise(n)
                unit()
                t.tick("small0")
                t.tick("small1")
                if n == 0:
                    dve.wait_ge(consts, N_CONSTS)
                dve.wait_ge(small_free[0], t.value("small0"))
                dve.wait_ge(small_free[1], t.value("small1"))
                pool_group(n, w)
                dve.wait_ge(pscale_loaded, 16 * (n + 1))
                dve.wait_ge(unit_taken, t.value("unit"))
                dve.tensor_tensor(pscale[:, :], pscale[:, :], gate[:, :], ALU.mult).then_inc(pscale_ready, 1)
                chunk(HG)
                dve.wait_ge(pscale_ready, n + 1)
                dve.wait_ge(small_full[1], t.value("small1"))
                update(n % 2, n, pscale)
                t.tick("prod")
                t.tick("sq", TB)
            with t.loop(dve, NCH, PER_2UNITS):
                unit()
                unit()

            def take_value():
                dve.wait_ge(w_used, t.value("used"))
                dve.wait_ge(prod_free[0], t.value("prod", 0, 1, 2))
                dve.tensor_tensor(tok[:, :, :], tok[:, :, :], prod[1][:, :, :], ALU.mult).then_inc(prod_free[1], 1)

            def low_hidden(at, half):
                t.tick(f"small{half}")
                t.tick("hid")
                dve.wait_ge(ghi_ready, t.value("hid"))
                blocks = bass.ds(at + 2 * half, 2)
                dve.tensor_tensor(g_lo[:, blocks, :], small[half][:, :].rearrange("p (a s) -> p a s", a=2),
                                  g_hi[:, blocks, :], ALU.subtract).then_inc(small_free[half], 1)

            def ffn_pair(at, first, units):
                def in_gate(k):
                    if k == EVAC - 1 and not first:
                        take_value()
                    for span in units:
                        for b in due(k, KD, *span):
                            fold(b)
                    if k == TURN + 3 and not first:
                        low_hidden(at, 0)
                    if k == TURN + 4 and not first:
                        low_hidden(at, 1)

                def in_value(k):
                    for span in units:
                        for b in due(k + KD, KD, *span):
                            fold(b)

                chunk(KD, in_gate)
                chunk(KD, in_value)
                t.tick("prod", 2)

            def ffn_out(layer):
                spans = OUT_UNITS[2 - layer]
                with t.loop(dve, NCH // 2, dict(PER_OUT[2 - layer], used=2 * KF)) as i:
                    for o in range(2):
                        def in_out(k):
                            if k == EVAC + 1 and o == 1:
                                update(0, i * 2, gate, len(spans) - 1)
                            for span in spans:
                                for b in due(k, KD, *span):
                                    fold(b)
                        chunk(KF, in_out)
                    update(1, i * 2 + 1, gate, len(spans) - 1)
                    t.tick("prod", 2)
                    t.tick("sq", 2 * TB)

            features(C_GFFN, 1)
            ffn_pair(0, True, FIRST_UNITS)
            with t.loop(dve, 2 * NCH - 1, dict(PER_IN_UNIT, used=2 * KD)) as i:
                ffn_pair(i * HG, False, [IN_UNIT])
            with t.loop(dve, NF - 2 * NCH, dict(PER_IN_UNIT, used=2 * KD)) as i:
                ffn_pair(i * HG + (2 * NCH - 1) * HG, False, [IN_UNIT])
            take_value()
            low_hidden((NF - 1) * HG, 0)
            low_hidden((NF - 1) * HG, 1)
            ffn_out(0)

            features(C_GMIX + KD, 0)
            dve.wait_ge(hgrn_consts, N_HGRN_CONSTS)
            b4 = lambda a, h: a.rearrange("p a s -> p (a s)").rearrange("p (n two h) -> p n two h", two=2, h=h)

            def forget(i):
                for half in range(2):
                    t.tick(f"small{half}")
                    dve.wait_ge(small_free[half], t.value(f"small{half}"))
                for hd in range(HG):
                    ins = dve.tensor_scalar(fT[:, hd], fT[:, hd], upper[:, bass.ds(i * HG + hd, 1)],
                                            lower[:, bass.ds(i * HG + hd, 1)], ALU.mult, ALU.add)
                ins.then_inc(fT_ready, 1)
                t.tick("bs")
                dve.wait_ge(fT_ready, t.value("bs"))
                dve.tensor_scalar(kT[:, :, :], fT[:, :, :], -1.0, 1.0, ALU.mult, ALU.add)
                dve.tensor_scalar(dec[:, 0], fT[:, :, :], LN_FLOOR, None, ALU.max).then_inc(f_ready, 1)

            def cumulate():
                t.tick("logs")
                dve.wait_ge(log_ready, t.value("logs"))
                dve.tensor_tensor_scan(bT[:, :, :].rearrange("p a s -> p (a s)"), keep[:, :],
                                       dec[:, 1].rearrange("p a s -> p (a s)"), 0.0, ALU.mult, ALU.add).then_inc(b_ready, 1)

            def exponents(j):
                d = dec[:, j % 2]
                if j == 0:
                    dve.wait_ge(b_ready, t.value("group", 1))
                    ref = bT[:, :, P - 1:P].to_broadcast([P, HG, P])
                    dve.tensor_tensor(d[:, :, 0:P], ref, bT[:, :, 0:P], ALU.subtract)
                    dve.tensor_copy(d[:, :, P:], bT[:, :, P:]).then_inc(arg_ready, 1)
                    return
                h = LEVELS[j - 1]
                b, e = b4(bT[:, :, :], h), b4(d, h)
                ref = b[:, :, 0, h - 1:h].to_broadcast([P, HG * S // (2 * h), h])
                dve.tensor_tensor(e[:, :, 0], ref, b[:, :, 0], ALU.subtract)
                dve.tensor_tensor(e[:, :, 1], b[:, :, 1], ref, ALU.subtract).then_inc(arg_ready, 1)

            def decayed(j):
                t.tick("level")
                dve.wait_ge(dec_ready, t.value("level"))
                d, kd, qd = dec[:, j % 2], kdec[:, j % 2], qdec[:, j % 2]
                if j == 0:
                    dve.tensor_tensor(kd[:, :, 0:P], kT[:, :, 0:P], d[:, :, 0:P], ALU.mult)
                    dve.tensor_tensor(qd, qT[:, :, P:], d[:, :, P:], ALU.mult).then_inc(qk_ready, 1)
                    return
                h = LEVELS[j - 1]
                dve.tensor_tensor(b4(kd, h)[:, :, 0], b4(kT[:, :, :], h)[:, :, 0], b4(d, h)[:, :, 0], ALU.mult)
                dve.tensor_tensor(qd.rearrange("p a s -> p (a s)").rearrange("p (n h) -> p n h", h=h),
                                  b4(qT[:, :, :], h)[:, :, 1], b4(d, h)[:, :, 1], ALU.mult).then_inc(qk_ready, 1)

            def scores(k):
                bk = k % 2
                t.tick(f"small{bk}")
                dve.wait_ge(small_full[bk], t.value(f"small{bk}"))
                if k < 2:
                    dve.tensor_tensor(sdiag[:, 2 * k:2 * k + 2].rearrange("p a b s -> p (a b) s"),
                                      small[bk][:, :].rearrange("p (n s) -> p n s", s=P),
                                      ident[:, :].unsqueeze(1).to_broadcast([P, 2 * TB, P]), ALU.mult).then_inc(small_free[bk], 1)
                    return
                if k == 2:
                    dve.tensor_copy(scross[:, :, :].rearrange("p a s -> p (a s)"), small[bk][:, :]).then_inc(small_free[bk], 1)
                    return
                h = LEVELS[k - 3]
                m = masks[:, k - 3, :].unsqueeze(1).to_broadcast([P, HG * TB, P // 2])
                if k > 3:
                    dve.wait_ge(s_masked, t.value("sm"))
                dve.tensor_tensor(smask[:, :, :], small[bk][:, :].rearrange("p (n s) -> p n s", s=P // 2), m,
                                  ALU.mult).then_inc(small_free[bk], 1)
                dve.wait_ge(small_free[bk], t.value(f"small{bk}"))
                if k == 3:
                    dve.wait_ge(small_free[1], t.value("small1", -1))
                target = b4(sdiag[:, :, :, :].rearrange("p a b s -> p (a b) s"), h)[:, :, 1]
                dve.tensor_tensor(target, target, smask[:, :, :].rearrange("p n s -> p (n s)").rearrange("p (n h) -> p n h", h=h),
                                  ALU.add).then_inc(s_ready if k == NL - 1 else s_masked, 1)
                if k < NL - 1:
                    t.tick("sm")

            def in_q(k):
                if k == TURN + 3:
                    forget(i)
                if k == TURN + 7:
                    cumulate()

            def in_vg(k):
                for j in range(NL - 2):
                    at = LEVEL_AT + LEVEL_EVERY * j
                    if k == at:
                        exponents(j)
                    if k == at + 2:
                        decayed(j)
                if k == LEVEL_AT + 1:
                    for half in range(2):
                        t.tick(f"small{half}")
                        dve.wait_ge(small_free[half], t.value(f"small{half}"))
                if k in (LEVEL_AT + 3, LEVEL_AT + 4):
                    scores(k - LEVEL_AT - 3)
                for j in range(NL - 2):
                    if k == LEVEL_AT + LEVEL_EVERY * j + 5:
                        scores(2 + j)

            with t.loop(dve, NCH, dict(PER_HGRN, used=4 * KD, bs=1, logs=1, sm=NL - 4, ov=2)) as i:
                chunk(KD, None, True)
                chunk(KD, in_q, True)
                chunk(KD, in_vg, True)
                chunk(KD, lambda k: in_vg(k + KD), True)
                for k in range(2 * KD, LEVEL_AT + LEVEL_EVERY * (NL - 3) + 6):
                    in_vg(k)
                t.tick("prod", 4)
                t.tick("group")
                for tb in range(TB):
                    t.tick(f"small{tb}")
                dve.wait_ge(osq_ready, t.value("group", 0, TB))
                dve.tensor_reduce(hn[:, :, :].rearrange("p a b -> p (a b)"),
                                  sq[:, :, :].rearrange("p a (b s) -> p (a b) s", s=P), AXX, ALU.add).then_inc(ovar_step, 1)
                t.tick("ov")
                dve.wait_ge(ovar_step, t.value("ov"))
                dve.tensor_scalar(hn[:, :, :], hn[:, :, :], 1.0 / P, EPS, ALU.mult, ALU.add).then_inc(ovar_step, 1)
                t.tick("ov")
                dve.wait_ge(ovar_step, t.value("ov"))
                dve.reciprocal(hn[:, :, :], hn[:, :, :]).then_inc(ovar_ready, 1)
                dve.wait_ge(orstd_ready, t.value("group"))
                for tb in range(TB):
                    o = og[:, tb, bass.ds(i * CH, CH)].rearrange("p (b s) -> p b s", s=P)
                    dve.tensor_tensor(o, small[tb][:, :].rearrange("p (b s) -> p b s", s=P),
                                      hn[:, tb].unsqueeze(2).to_broadcast([P, HG, P]), ALU.mult).then_inc(small_free[tb], 1)
                for tb in range(TB):
                    dve.wait_ge(small_free[tb], t.value(f"small{tb}"))
                dve.wait_ge(prod_free[1], t.value("prod", 0, 1, 2))
                o = og[:, :, bass.ds(i * CH, CH)]
                dve.tensor_tensor(o, o, sg[:, :, :], ALU.mult).then_inc(og_ready, 1)
            for n in range(NCH):
                split_feat(n)
            with t.loop(dve, NCH // 2, dict(PER_WOUT, used=2 * KD)) as i:
                def in_wout(k):
                    for b in due(k, KD, *WOUT_UNIT):
                        fold(b)

                def in_second(k):
                    if k == EVAC + 2:
                        update(0, i * 2)
                    in_wout(k)

                chunk(KD, in_wout)
                chunk(KD, in_second)
                update(1, i * 2 + 1)
                t.tick("prod", 2)
                t.tick("sq", 2 * TB)
            features(C_GFFN + KD, 1)
            ffn_pair(0, True, [])
            with t.loop(dve, NF - 1, dict(PER_IN, used=2 * KD)) as i:
                ffn_pair(i * HG, False, [])
            take_value()
            low_hidden((NF - 1) * HG, 0)
            low_hidden((NF - 1) * HG, 1)
            ffn_out(1)
            norm_prepare(None, 0)
            dve.wait_ge(fgain_loaded, 16)
            for tb in range(TB):
                dve.scalar_tensor_tensor(xs[:, tb], xs[:, tb], rstd[:, tb:tb + 1], fgain, ALU.mult, ALU.mult).then_inc(y_ready, 1)


_NAMES = ["x", "c", "norm_mix_gain", "norm_ffn_gain", "w_ada", "b_ada", "pool_w", "pool_scale", "hgrn_w_in",
          "hgrn_w_out", "hgrn_norm_gain", "hgrn_lb", "w_ffn_in", "w_ffn_out", "final_gain"]


def kernel(**inputs):
    import concourse.bacc as bacc
    from concourse.bass_utils import run_bass_kernel_spmd

    nc = bacc.Bacc("TRN2", target_bir_lowering=False, num_devices=1)
    arrays, args = {}, []
    for name in _NAMES:
        a = np.ascontiguousarray(inputs[name])
        arrays[f"in_{name}"] = a
        args.append(nc.dram_tensor(f"in_{name}", a.shape, mybir.dt.from_np(a.dtype), kind="ExternalInput").ap())
    out = nc.dram_tensor("out", inputs["x"].shape, F32, kind="ExternalOutput").ap()
    build(nc, *args, out)
    result = run_bass_kernel_spmd(nc, [arrays], core_ids=[0])
    return result.results[0]["out"]
```

```python
from contextlib import ExitStack, contextmanager

import numpy as np
import concourse.bass as bass
from concourse import mybir

F32 = mybir.dt.float32
F32R = mybir.dt.float32r
BF16 = mybir.dt.bfloat16
ALU = mybir.AluOpType
ACT = mybir.ActivationFunctionType
AXX = mybir.AxisListType.X

P = 128
CH = 512
EPS = 1e-6
WINDOWS = (2, 4, 8, 16)
PAD = 16
LEVELS = (64, 32, 16, 8, 4, 2, 1)
LN_FLOOR = 2.0 ** -60


class Tally:

    def __init__(self):
        self.n = {}
        self.i = None
        self.first = 0
        self.per = {}

    def some(self, name, n=1):
        return self.get(name) >= n

    def get(self, name):
        return self.n.get(name, 0)

    def tick(self, name, k=1):
        self.n[name] = self.get(name) + k

    def value(self, name, add=0, scale=1, div=1):
        const = scale * (self.get(name) // div + add)
        if self.i is None or not self.per.get(name, 0):
            return const
        assert self.per[name] % div == 0
        step = scale * self.per[name] // div
        return self.i * step + (const - self.first * step)

    @contextmanager
    def loop(self, eng, count, per, first=0):
        before = dict(self.n)
        with eng.Fori(first, first + count) as i:
            self.i, self.first, self.per = i, first, per
            yield i
        for name in list(self.n):
            grown = self.get(name) - before.get(name, 0)
            assert grown in (0, per.get(name, 0)), (name, grown, per.get(name, 0))
            self.n[name] = before.get(name, 0) + count * grown
        self.i, self.per = None, {}


def due(step, n, first, last):
    return [k for k in range(n) if first + k * (last - first + 1) // n == step]


def build(nc, x, c, norm_mix_gain, norm_ffn_gain, w_ada, b_ada, pool_w, pool_scale, hgrn_w_in,
          hgrn_w_out, hgrn_norm_gain, hgrn_lb, w_ffn_in, w_ffn_out, final_gain, out):
    D = x.shape[2]
    TB = x.shape[1] // P
    S = TB * P
    KD = D // P
    NCH = D // CH
    F = w_ffn_out.shape[1]
    KF = F // P
    NF = F // CH
    HG = CH // P
    KU = KD // 2
    NL = 3 + len(LEVELS)
    RAW = 4
    SPL = 4
    ADA = 4
    AHEAD = SPL
    assert AHEAD == HG

    EVAC = 3
    TURN = 6
    IN_UNIT = (0, 24)
    FIRST_UNITS = [(4, 14), (16, 27)]
    OUT_UNITS = {1: [(0, 31)], 2: [(0, 15), (20, 35)]}
    WOUT_UNIT = (3, 13)
    SUM = 2
    LEVEL_AT, EVERY, EVERY_LAST, O_AT = 8, 5, 3, 3 * KD + 3

    def per(steps, chunks, units=0, **more):
        return dict(step=steps, raw=steps // 2, prod=chunks, unit=units, ada=KU * units, **more)

    PER_2UNITS = dict(unit=2, ada=2 * KU)
    PER_IN = per(2 * KD, 2, 0, small0=1, small1=1, hid=2)
    PER_IN_UNIT = per(2 * KD, 2, 1, small0=1, small1=1, hid=2)
    PER_OUT = {n: per(2 * KF, 2, 2 * n, upd=2, sq=2 * TB) for n in (1, 2)}
    PER_WOUT = per(2 * KD, 2, 2, upd=2, sq=2 * TB)
    PER_HGRN = per(4 * KD, 4, 0, small0=3 + NL // 2, small1=3 + NL // 2, level=NL - 2, group=1, forget=1)

    CLOSE = 5 * NCH

    def unit_buffer(t):
        return t.get("unit") % 2 if t.get("unit") < CLOSE else 0

    def unit_parts(t):
        return 2 if t.get("unit") < CLOSE else 1

    def unit_lag(t):
        return 1 if t.get("unit") < CLOSE else 0

    ctx = ExitStack()
    with ctx:
        def sb(name, shape, dt=F32, where=ctx):
            return where.enter_context(nc.sbuf_tensor(name, shape, dt))

        def sem(name):
            return ctx.enter_context(nc.semaphore(name))

        xs = sb("xs", [P, TB, D])
        h_hi = sb("h_hi", [P, KD, S], F32R)
        h_lo = sb("h_lo", [P, KD, S], F32R)
        raw = sb("raw", [P, RAW, 2, CH])
        w_hi = sb("w_hi", [P, SPL, CH], F32R)
        w_lo = sb("w_lo", [P, SPL, CH], F32R)
        ada = sb("ada", [P, ADA, 2, CH])
        acc = sb("acc", [P, 2, CH]) 
        bias = sb("bias", [1, CH])
        gate = sb("gate", [P, CH])
        tok = sb("tok", [P, TB, CH])
        feat = sb("feat", [P, 2, 2, S])
        junk = sb("junk", [P, CH], BF16)
        ident = sb("ident", [P, P])
        ones = sb("ones", [P, P])
        cols = sb("cols", [P, P])
        cond = sb("cond", [P, KD])
        mod = sb("mod", [P, 2, 2 * KD])
        gain = sb("gain", [P, KD])
        zero = sb("zero", [P, KD])
        lower = sb("lower", [P, KD])
        upper = sb("upper", [P, KD])
        ssq = sb("ssq", [P, TB, NCH])
        rstd = sb("rstd", [P, TB])

        with ExitStack() as pooling:
            rows = sb("rows", [P, P], where=pooling)
            pscale = sb("pscale", [P, CH], where=pooling)
            padded = sb("padded", [P, HG, PAD + S], where=pooling)
            win = [sb(f"win{i}", [P, HG, PAD + S], where=pooling) for i in range(2)]
            diff = sb("diff", [P, HG, S], where=pooling)
            edge = sb("edge", [P, HG, PAD], where=pooling)
            inv = sb("inv", [P, PAD], where=pooling)
            lbt = sb("lbt", [P, 4, KD], where=pooling)
        with ExitStack() as hgrn:
            keep = sb("keep", [P, HG * S], BF16, where=hgrn)
            masks = sb("masks", [P, len(LEVELS), P // 2], where=hgrn)
            fT = sb("fT", [P, HG, S], where=hgrn)
            kT = sb("kT", [P, HG, S], where=hgrn)
            bT = sb("bT", [P, HG, S], where=hgrn)
            qT = sb("qT", [P, HG, S], where=hgrn)
            dec = sb("dec", [P, 2, HG, S], where=hgrn)
            kdec = sb("kdec", [P, 2, HG, S], where=hgrn)
            qdec = sb("qdec", [P, 2, HG, P], where=hgrn)
            sdiag = sb("sdiag", [P, HG, TB, P], where=hgrn)
            scross = sb("scross", [P, HG, P], where=hgrn)
            smask = sb("smask", [P, HG * TB, P // 2], where=hgrn)
            vt = sb("vt", [P, TB, CH], where=hgrn)
            sg = sb("sg", [P, TB, CH], where=hgrn)
            hn = sb("hn", [P, TB, HG], where=hgrn)
            og = sb("og", [P, TB, D], where=hgrn)
            w_hi2 = sb("w_hi2", [P, SPL, CH], F32R, where=hgrn)
            w_lo2 = sb("w_lo2", [P, SPL, CH], F32R, where=hgrn)
        g_hi = sb("g_hi", [P, KF, S], F32R)
        g_lo = sb("g_lo", [P, KF, S], F32R)
        sq = fT[:, :, :].rearrange("p a s -> p (a s)").rearrange("p (t n) -> p t n", t=TB)
        accs = [acc, feat[:, :, :, :].rearrange("p a b s -> p a (b s)")]
        fgain = ada[:, 0:2].rearrange("p a b n -> p (a b n)")

        prod = [ctx.enter_context(nc.psum_tensor(f"prod{i}", [P, TB, CH], F32)) for i in range(2)]
        small = [ctx.enter_context(nc.psum_tensor(f"small{i}", [P, CH], F32)) for i in range(2)]
        modp = ctx.enter_context(nc.psum_tensor("modp", [P, CH], F32))

        C_GMIX, C_GFFN, C_HGAIN, C_LB = KD, 3 * KD, 5 * KD, 6 * KD

        raw_loaded = [sem(f"raw_loaded{i}") for i in range(RAW)]
        ada_loaded = [sem(f"ada_loaded{i}") for i in range(ADA)]
        params_loaded = sem("params_loaded")
        x_loaded = sem("x_loaded")
        bias_loaded = sem("bias_loaded")
        pscale_loaded = sem("pscale_loaded")
        fgain_loaded = sem("fgain_loaded")
        stored = sem("stored")
        consts = sem("consts")
        hgrn_consts = sem("hgrn_consts")
        w_used = sem("w_used")
        unit_reduced = sem("unit_reduced")
        small_full = [sem(f"small_full{i}") for i in range(2)]
        hi_ready = sem("hi_ready")
        unit_taken = sem("unit_taken")
        cond_ready = sem("cond_ready")
        lb_exp = sem("lb_exp")
        squared = sem("squared")
        rstd_ready = sem("rstd_ready")
        ghi_ready = sem("ghi_ready")
        log_ready = sem("log_ready")
        dec_ready = sem("dec_ready")
        osq_ready = sem("osq_ready")
        orstd_ready = sem("orstd_ready")
        lo_ready = sem("lo_ready")
        ada_half = sem("ada_half")
        ada_used = sem("ada_used")
        unit_summed = sem("unit_summed")
        cols_ready = sem("cols_ready")
        lb_max = sem("lb_max")
        lb_ready = sem("lb_ready")
        var_step = sem("var_step")
        var_ready = sem("var_ready")
        tok_ready = sem("tok_ready")
        h_high = sem("h_high")
        h_ready = sem("h_ready")
        pool_step = sem("pool_step")
        pscale_ready = sem("pscale_ready")
        x_updated = sem("x_updated")
        f_ready = sem("f_ready")
        fT_ready = sem("fT_ready")
        b_ready = sem("b_ready")
        arg_ready = sem("arg_ready")
        qk_ready = sem("qk_ready")
        s_masked = sem("s_masked")
        s_ready = sem("s_ready")
        ovar_step = sem("ovar_step")
        ovar_ready = sem("ovar_ready")
        og_ready = sem("og_ready")
        final_step = sem("final_step")
        y_ready = sem("y_ready")
        prod_free = [sem(f"prod_free{i}") for i in range(2)]
        small_free = [sem(f"small_free{i}") for i in range(2)]

        def split_slot(t, deep):
            k = t.get("step") % (2 * SPL if deep else SPL)
            return (w_hi[:, k], w_lo[:, k]) if k < SPL else (w_hi2[:, k - SPL], w_lo2[:, k - SPL])

        block = ctx.enter_context(nc.Block())
        FFN_STEPS = 2 * KD * NF + KF * NCH

        @block.sync
        def _(sp):
            t = Tally()

            def load_w(src):
                slot = t.get("raw") % RAW
                if t.some("raw", RAW):
                    sp.wait_ge(lo_ready, t.value("raw", 1 - RAW, 2))
                sp.dma_start(raw[:, slot], src.rearrange("(a p) n -> p a n", p=P)).then_inc(raw_loaded[slot], 16)
                t.tick("raw")

            def load_ada(layer, at, k):
                if k == ADA:
                    if t.some("unit"):
                        sp.wait_ge(unit_summed, t.value("unit"))
                    sp.dma_start(bias[:, :], b_ada[layer:layer + 1, bass.ds(at, CH)]).then_inc(bias_loaded, 16)
                slot = t.get("ada") % ADA
                if t.some("ada", ADA):
                    sp.wait_ge(ada_used, t.value("ada", 1 - ADA))
                src = w_ada[layer, 2 * k * P:2 * (k + 1) * P, bass.ds(at, CH)]
                sp.dma_start(ada[:, slot], src.rearrange("(a p) n -> p a n", p=P)).then_inc(ada_loaded[slot], 16)
                t.tick("ada")
                if k == KU - 1:
                    t.tick("unit")

            def load_unit(layer, at):
                for k in range(KU):
                    load_ada(layer, at, k)

            def load_chunk(src, at, blocks, units=(), shift=0, loaded=0):
                for s in range(blocks):
                    if s % 2 == 0 and s >= loaded:
                        load_w(src[s * P:(s + 2) * P, bass.ds(at, CH)])
                    for layer, col, span in units:
                        for k in due(s + shift, KU, *span):
                            load_ada(layer, col, k)

            at = 0
            for src in (c, norm_mix_gain, norm_ffn_gain, hgrn_norm_gain, hgrn_lb):
                n = src.shape[0] * KD
                sp.dma_start(rows[at:at + n, :], src.rearrange("l (k p) -> (l k) p", p=P)).then_inc(params_loaded, 16)
                at += n
            for tb in range(TB):
                sp.dma_start(xs[:, tb], x[0, tb * P:(tb + 1) * P, :]).then_inc(x_loaded, 16)
            load_unit(0, 0)
            load_unit(0, CH)
            with t.loop(sp, NCH - 1, PER_2UNITS) as i:
                load_unit(0, i * 2 * CH + 2 * CH)
                load_unit(0, i * 2 * CH + 3 * CH)
            for n in range(NCH):
                load_chunk(pool_w[0, n], 0, HG)
                load_unit(0, 2 * D + n * CH)
                if n:
                    sp.wait_ge(x_updated, n)
                sp.dma_start(pscale[:, :], pool_scale[0:1, n * CH:(n + 1) * CH].to_broadcast([P, CH])).then_inc(pscale_loaded, 16)
            load_chunk(w_ffn_in[0], 0, AHEAD)
            with t.loop(sp, NCH, PER_2UNITS) as i:
                load_unit(0, i * 2 * CH + 3 * D)
                load_unit(0, i * 2 * CH + (3 * D + CH))

            def load_pair(at, units, loaded=0):
                load_chunk(w_ffn_in[0 if units is not None else 1], at, KD, units or (), 0, loaded)
                load_chunk(w_ffn_in[0 if units is not None else 1], at + F, KD, units or (), KD)

            def load_ffn_out(layer):
                with t.loop(sp, NCH // 2, PER_OUT[2 - layer]) as i:
                    for o in range(2):
                        units = [(layer, i * 2 * CH + (5 * D + o * CH)), (1, i * 2 * CH + (3 * D + o * CH))]
                        load_chunk(w_ffn_out[layer], i * 2 * CH + o * CH, KF,
                                   [(*unit, span) for unit, span in zip(units, OUT_UNITS[2 - layer])])

            load_pair(0, [(1, 0, FIRST_UNITS[0]), (1, 4 * D, FIRST_UNITS[1])], AHEAD)
            with t.loop(sp, 2 * NCH - 1, PER_IN_UNIT) as i:
                load_pair(i * CH + CH, [(1, i * CH + CH, IN_UNIT)])
            with t.loop(sp, NF - 2 * NCH, PER_IN_UNIT) as i:
                load_pair(i * CH + 2 * NCH * CH, [(1, i * CH + (4 * D + CH), IN_UNIT)])
            load_ffn_out(0)
            load_chunk(hgrn_w_in[0], D, KD)
            load_chunk(hgrn_w_in[0], 0, KD)
            with t.loop(sp, NCH - 1, PER_HGRN) as i:
                load_chunk(hgrn_w_in[0], i * CH + 2 * D, KD)
                load_chunk(hgrn_w_in[0], i * CH + 3 * D, KD)
                load_chunk(hgrn_w_in[0], i * CH + (D + CH), KD)
                load_chunk(hgrn_w_in[0], i * CH + CH, KD)
            load_chunk(hgrn_w_in[0], 2 * D + (NCH - 1) * CH, KD)
            load_chunk(hgrn_w_in[0], 3 * D + (NCH - 1) * CH, KD)
            with t.loop(sp, NCH // 2, PER_WOUT) as i:
                for o in range(2):
                    load_chunk(hgrn_w_out[0], i * 2 * CH + o * CH, KD,
                               [(1, i * 2 * CH + (2 * D + o * CH), WOUT_UNIT)])
            with t.loop(sp, NF, PER_IN) as i:
                load_pair(i * CH, None)
            load_ffn_out(1)
            sp.wait_ge(ada_used, t.value("ada"))
            sp.dma_start(fgain, final_gain.rearrange("(a n) -> a n", a=1).to_broadcast([P, D])).then_inc(fgain_loaded, 16)
            for tb in range(TB):
                sp.wait_ge(y_ready, tb + 1)
                sp.dma_start(out[0, tb * P:(tb + 1) * P, :], xs[:, tb]).then_inc(stored, 16)
            sp.wait_ge(stored, 16 * TB)

        N_CONSTS = 4 + PAD + 1
        N_HGRN_CONSTS = 4 + 2 * len(LEVELS)

        @block.gpsimd
        def _(pool):
            pool.memset(ident[:, :], 0.0).then_inc(consts, 1)
            pool.memset(ones[:, :], 1.0).then_inc(consts, 1)
            pool.memset(zero[:, :], 0.0).then_inc(consts, 1)
            pool.memset(padded[:, :, 0:PAD], 0.0).then_inc(consts, 1)
            for n in range(PAD):
                pool.memset(inv[:, n:n + 1], 1.0 / (n + 1)).then_inc(consts, 1)
            pool.wait_ge(consts, 4 + PAD)
            pool.affine_select(out=ident[:, :], in_=ident[:, :], compare_op=ALU.not_equal, fill=1.0,
                               base=0, pattern=[[-1, P]], channel_multiplier=1).then_inc(consts, 1)
            pool.wait_ge(w_used, HG * NCH + FFN_STEPS)
            pool.memset(keep[:, :], 1.0).then_inc(hgrn_consts, 1)
            pool.memset(masks[:, :, :], 1.0).then_inc(hgrn_consts, 1)
            pool.memset(kdec[:, :, :, :], 0.0).then_inc(hgrn_consts, 1)
            pool.wait_ge(hgrn_consts, 3)
            pool.memset(keep[:, :].rearrange("p (n c) -> p n c", c=P)[:, :, 0:1], 0.0).then_inc(hgrn_consts, 1)
            for j, h in enumerate(LEVELS):
                m = masks[:, j, :].rearrange("p (b o) -> p b o", o=h)
                pool.affine_select(out=m, in_=m, compare_op=ALU.is_ge, fill=0.0, base=0,
                                   pattern=[[-2 * h, P // (2 * h)], [0, h]], channel_multiplier=1).then_inc(hgrn_consts, 1)
            pool.wait_ge(hgrn_consts, 4 + len(LEVELS))
            for j, h in enumerate(LEVELS):
                m = masks[:, j, :].rearrange("p (b o) -> p b o", o=h)
                pool.affine_select(out=m, in_=m, compare_op=ALU.is_ge, fill=0.0, base=h - 1,
                                   pattern=[[2 * h, P // (2 * h)], [0, h]], channel_multiplier=-1).then_inc(hgrn_consts, 1)

        @block.tensor
        def _(pe):
            t = Tally()

            def bank(n):
                if t.some(f"small{n}"):
                    pe.wait_ge(small_free[n], t.value(f"small{n}"))

            def filled(ins, n):
                ins.then_inc(small_full[n], 1)
                t.tick(f"small{n}")

            def product(hi, lo, blocks, after=None, deep=False, before=None):
                par = t.get("prod") % 2
                if t.some("prod", 2):
                    pe.wait_ge(prod_free[par], t.value("prod", 0, 1, 2))
                for k in range(blocks):
                    if before is not None:
                        before(k)
                    wh, wl = split_slot(t, deep)
                    pe.wait_ge(lo_ready, t.value("step", 1))
                    for tb in range(TB):
                        ts = slice(tb * P, (tb + 1) * P)
                        o = prod[par][:, tb]
                        pe.matmul(o, hi(k)[:, ts], wh, start=(k == 0), stop=False)
                        pe.matmul(o, hi(k)[:, ts], wl, start=False, stop=False)
                        mm = pe.matmul(o, lo(k)[:, ts], wh, start=False, stop=(k == blocks - 1))
                    mm.then_inc(w_used, 1)
                    t.tick("step")
                    if after is not None:
                        after(k)
                t.tick("prod")

            def h_product(after=None, deep=False, before=None):
                product(lambda k: h_hi[:, k], lambda k: h_lo[:, k], KD, after, deep, before)

            def reduce_unit(rowwise):
                a, parts = accs[unit_buffer(t)], unit_parts(t)
                pe.wait_ge(unit_summed, t.value("unit", 1))
                if t.some("unit"):
                    pe.wait_ge(unit_taken, t.value("unit"))
                if rowwise:
                    for par in range(parts):
                        mm = pe.matmul(modp[:, :], ones[:, :], a[:, par], start=(par == 0), stop=(par == parts - 1))
                else:
                    for j in range(HG):
                        for par in range(parts):
                            mm = pe.matmul(modp[:, j:j + 1], a[:, par, j * P:(j + 1) * P], ones[:, 0:1],
                                           start=(par == 0), stop=(par == parts - 1))
                mm.then_inc(unit_reduced, 1)
                t.tick("unit")

            def turn(block_of):
                for half in range(2):
                    bank(half)
                    for j in range(2):
                        for tb in range(TB):
                            o = (j * TB + tb) * P
                            mm = pe.transpose(small[half][:, o:o + P], block_of(tb, 2 * half + j), ident[:, :])
                    filled(mm, half)

            def turn_tok():
                turn(lambda tb, b: tok[:, tb, b * P:(b + 1) * P])

            def turn_normalised():
                t.tick("tok")
                pe.wait_ge(tok_ready, t.value("tok"))
                turn_tok()

            def features(k):
                if k == 0:
                    turn_normalised()
                if k % HG == 0 and k // HG + 1 < NCH:
                    turn_normalised()
                if k % 2 == 0:
                    t.tick("h")
                    pe.wait_ge(h_ready, t.value("h"))

            pe.wait_ge(consts, N_CONSTS)
            pe.wait_ge(params_loaded, 16 * 5)
            filled(pe.transpose(small[0][:, 0:P], rows[:, :], ident[:, :]), 0)
            reduce_unit(False)
            reduce_unit(False)
            with t.loop(pe, NCH - 1, PER_2UNITS):
                reduce_unit(False)
                reduce_unit(False)
            for n in range(NCH):
                turn_normalised()
                t.tick("h", 2)
                pe.wait_ge(h_ready, t.value("h"))
                product(lambda k: h_hi[:, n * HG + k], lambda k: h_lo[:, n * HG + k], HG)
                reduce_unit(True)
            with t.loop(pe, NCH, PER_2UNITS):
                reduce_unit(False)
                reduce_unit(False)

            def turn_hidden():
                pe.wait_ge(prod_free[1], t.value("prod", 0, 1, 2))
                turn_tok()

            def ffn_pair(first, units):
                def in_gate(k):
                    if k == TURN and not first:
                        turn_hidden()
                    if k in [last + SUM for _, last in units]:
                        reduce_unit(False)

                def in_value(k):
                    if k + KD in [last + SUM for _, last in units]:
                        reduce_unit(False)

                h_product(in_gate, False, features if first else None)
                h_product(in_value)

            def ffn_out(layer):
                spans = OUT_UNITS[2 - layer]

                def in_out(k):
                    if k == spans[0][1] + SUM:
                        reduce_unit(True)
                    if layer == 0 and k == spans[1][1] + SUM:
                        reduce_unit(False)

                def last_hidden(k):
                    if k == KF - HG:
                        pe.wait_ge(small_free[0], t.value("small0"))
                        pe.wait_ge(small_free[1], t.value("small1"))

                with t.loop(pe, NCH // 2, PER_OUT[2 - layer]):
                    for o in range(2):
                        product(lambda k: g_hi[:, k], lambda k: g_lo[:, k], KF, in_out, False, last_hidden)

            ffn_pair(True, FIRST_UNITS)
            with t.loop(pe, NF - 1, PER_IN_UNIT):
                ffn_pair(False, [IN_UNIT])
            turn_hidden()
            ffn_out(0)

            def self_scores(k):
                bank(k)
                pe.wait_ge(b_ready, t.value("group", 1))
                if k == 0:
                    pe.wait_ge(small_free[1], t.value("small1"))
                for hd in (2 * k, 2 * k + 1):
                    for blk in range(TB):
                        o = ((hd % 2) * TB + blk) * P
                        ts = slice(blk * P, (blk + 1) * P)
                        mm = pe.matmul(small[k][:, o:o + P], kT[:, hd, ts], qT[:, hd, ts], start=True, stop=True)
                filled(mm, k)

            def level_scores(j):
                b, H = j % 2, P // 2
                bank(b)
                t.tick("level")
                pe.wait_ge(qk_ready, t.value("level"))
                for hd in range(HG):
                    if j == 0:
                        mm = pe.matmul(small[b][:, hd * P:(hd + 1) * P], kdec[:, b, hd, 0:P], qdec[:, b, hd, :],
                                       start=True, stop=True)
                        continue
                    for blk in range(TB):
                        o = (hd * TB + blk) * H
                        mm = pe.matmul(small[b][:, o:o + H], kdec[:, b, hd, blk * P:(blk + 1) * P],
                                       qdec[:, b, hd, blk * H:(blk + 1) * H], start=True, stop=True)
                filled(mm, b)

            def turn_forget(k):
                if k == TURN + 2:
                    pe.wait_ge(prod_free[0], t.value("prod", 1, 1, 2))
                    turn_tok()

            def output():
                t.tick("group")
                pe.wait_ge(s_ready, t.value("group"))
                pe.wait_ge(prod_free[0], t.value("prod", 0, 1, 2))
                for tb in range(TB):
                    bank(tb)
                    for hd in range(HG):
                        hs = slice(hd * P, (hd + 1) * P)
                        if tb:
                            pe.matmul(small[tb][:, hs], scross[:, hd], vt[:, 0, hs], start=True, stop=False)
                        mm = pe.matmul(small[tb][:, hs], sdiag[:, hd, tb], vt[:, tb, hs], start=(tb == 0), stop=True)
                    filled(mm, tb)

            def group_work(k, every):
                if k == TURN:
                    pe.wait_ge(prod_free[1], t.value("prod", 0, 1, 2))
                    turn_tok()
                if k in (TURN + 2, TURN + 3):
                    self_scores(k - TURN - 2)
                for j in range(NL - 2):
                    if k == LEVEL_AT + every * j + 2:
                        level_scores(j)
                if k == O_AT:
                    output()
                turn_forget(k - 3 * KD)

            assert t.get("step") % (2 * SPL) == 0
            h_product(None, True, features)
            h_product(turn_forget, True)
            with t.loop(pe, NCH - 1, PER_HGRN):
                for part in range(4):
                    h_product(lambda k: group_work(part * KD + k, EVERY), True)
            h_product(lambda k: group_work(k, EVERY_LAST), True)
            h_product(lambda k: group_work(KD + k, EVERY_LAST), True)
            for k in range(2 * KD, LEVEL_AT + EVERY_LAST * (NL - 3) + 3):
                group_work(k, EVERY_LAST)
            output()
            pe.wait_ge(og_ready, NCH)
            for n in range(NCH):
                turn(lambda tb, b: og[:, tb, (n * HG + b) * P:(n * HG + b + 1) * P])
            t.tick("h", 2 * NCH)
            pe.wait_ge(h_ready, t.value("h"))
            with t.loop(pe, NCH // 2, PER_WOUT):
                for o in range(2):
                    h_product()
                    reduce_unit(True)
            ffn_pair(True, [])
            with t.loop(pe, NF - 1, PER_IN):
                ffn_pair(False, [])
            turn_hidden()
            ffn_out(1)

        @block.scalar
        def _(act):
            t = Tally()

            def hi(deep=False):
                r = t.get("step") // 2 % RAW
                if t.get("step") % 2 == 0:
                    act.wait_ge(raw_loaded[r], t.value("step", 1, 16, 2 * RAW))
                if t.some("step", SPL):
                    act.wait_ge(w_used, t.value("step", 1 - (2 * SPL if deep else SPL)))
                act.activation(split_slot(t, deep)[0], raw[:, r, t.get("step") % 2], ACT.Copy).then_inc(hi_ready, 1)
                t.tick("step")

            def ahead():
                for k in range(AHEAD):
                    hi()

            def chunk(n, before=None, deep=False, done=0):
                for k in range(n):
                    if before is not None:
                        before(k)
                    if k >= done:
                        hi(deep)
                t.tick("used", n)

            def take_columns(dst):
                act.wait_ge(unit_reduced, t.value("unit", 1))
                act.activation(dst, modp[:, 0:HG], ACT.Copy).then_inc(unit_taken, 1)
                t.tick("unit")

            def take_gate():
                act.wait_ge(unit_reduced, t.value("unit", 1))
                if t.some("upd"):
                    act.wait_ge(x_updated, t.value("upd"))
                act.activation(gate[:, :], modp[:, :], ACT.Copy).then_inc(unit_taken, 1)
                t.tick("unit")

            def square(at):
                for tb in range(TB):
                    if t.some("sq"):
                        act.wait_ge(squared, t.value("sq"))
                    act.activation(junk[:, :], xs[:, tb, bass.ds(at * CH, CH)], ACT.Square,
                                   accum_out=ssq[:, tb, bass.ds(at, 1)]).then_inc(squared, 1)
                    t.tick("sq")

            def square_updated(at):
                t.tick("upd")
                act.wait_ge(x_updated, t.value("upd"))
                square(at)

            def root():
                t.tick("norm")
                act.wait_ge(var_ready, t.value("norm"))
                act.activation(rstd[:, :], rstd[:, :], ACT.Sqrt).then_inc(rstd_ready, 1)

            def filled(half):
                t.tick(f"small{half}")
                act.wait_ge(small_full[half], t.value(f"small{half}"))

            def modulate(gains, shifts, n, into=None):
                for half in range(2):
                    filled(half)
                    if into is None:
                        act.wait_ge(h_ready, t.value("h", -1))
                    for j in range(2):
                        k = n * HG + 2 * half + j
                        dst = feat[:, half, j] if into is None else into[:, 2 * half + j, PAD:]
                        ins = act.activation(dst, small[half][:, j * S:(j + 1) * S], ACT.Identity,
                                             bias=shifts[:, k:k + 1], scale=gains[:, k:k + 1])
                    ins.then_inc(small_free[half], 1)
                    t.tick("h")

            def features(k, gains, shifts):
                if k == 0:
                    modulate(gains, shifts, 0)
                    modulate(gains, shifts, 1)
                if k % HG == 0 and k // HG >= 2:
                    modulate(gains, shifts, k // HG)

            def take(par, dst, func):
                act.wait_ge(w_used, t.value("used"))
                act.activation(dst[:, :, :], prod[par][:, :, :], func).then_inc(prod_free[par], 1)

            act.wait_ge(cols_ready, 1)
            act.activation(cond[:, :], cols[:, 0:KD], ACT.Silu).then_inc(cond_ready, 1)
            act.wait_ge(x_loaded, 16 * TB)
            for n in range(NCH):
                square(n)
            act.wait_ge(lb_max, 3)
            act.activation(lbt[:, 2:4], lbt[:, 2:4], ACT.Exp).then_inc(lb_exp, 1)
            t.tick("small0")
            take_columns(mod[:, 0, 0:HG])
            take_columns(mod[:, 0, HG:2 * HG])
            with t.loop(act, NCH - 1, PER_2UNITS) as i:
                take_columns(mod[:, 0, bass.ds(i * 2 * HG + 2 * HG, HG)])
                take_columns(mod[:, 0, bass.ds(i * 2 * HG + 3 * HG, HG)])
            root()
            act.wait_ge(consts, N_CONSTS)
            for n in range(NCH):
                if n:
                    act.wait_ge(h_ready, 2 * n)
                modulate(gain, mod[:, 0, 0:KD], n, padded)
                chunk(HG)
                if n:
                    square_updated(n - 1)
                take_gate()
            square_updated(NCH - 1)
            with t.loop(act, NCH, PER_2UNITS) as i:
                take_columns(mod[:, 1, bass.ds(i * 2 * HG, HG)])
                take_columns(mod[:, 1, bass.ds(i * 2 * HG + HG, HG)])

            def take_hidden(at, half):
                filled(half)
                act.activation(g_hi[:, bass.ds(at + 2 * half, 2), :],
                               small[half][:, :].rearrange("p (a s) -> p a s", a=2), ACT.Copy).then_inc(ghi_ready, 1)

            def ffn_pair(at, first, units):
                def in_gate(k):
                    if first:
                        features(k, gain, mod[:, 1, 0:KD])
                    if k == TURN + 3 and not first:
                        take_hidden(at, 0)
                    if k == TURN + 4 and not first:
                        take_hidden(at, 1)

                def in_value(k):
                    if k == 6 and len(units) == 2:
                        take_columns(units[0])
                    if k == EVAC:
                        take(0, tok, ACT.Silu)

                chunk(KD, in_gate, False, AHEAD if first else 0)
                chunk(KD, in_value)
                if units:
                    take_columns(units[-1])

            def ffn_out(layer):
                spans = OUT_UNITS[2 - layer]
                def pair(i, end):
                    for o in range(2):
                        def in_out(k):
                            if k == EVAC + 3 and o == 1:
                                square_updated(i * 2)
                            if k == spans[0][1] + SUM + 4:
                                take_gate()
                            if layer == 0 and k == spans[1][1] + SUM + 4:
                                take_columns(mod[:, 1, bass.ds(i * 2 * HG + o * HG, HG)])
                        chunk(KF, in_out, False, AHEAD if o == 0 else 0)
                    if not end:
                        ahead()
                    square_updated(i * 2 + 1)

                with t.loop(act, NCH // 2 - layer, dict(PER_OUT[2 - layer], used=2 * KF)) as i:
                    pair(i, False)
                if layer:
                    pair(NCH // 2 - 1, True)

            ahead()
            root()
            ffn_pair(0, True, [mod[:, 0, 0:HG], mod[:, 1, KD:KD + HG]])
            with t.loop(act, 2 * NCH - 1, dict(PER_IN_UNIT, used=2 * KD)) as i:
                ffn_pair(i * HG, False, [mod[:, 0, bass.ds(i * HG + HG, HG)]])
            with t.loop(act, NF - 2 * NCH, dict(PER_IN_UNIT, used=2 * KD)) as i:
                ffn_pair(i * HG + (2 * NCH - 1) * HG, False, [mod[:, 1, bass.ds(i * HG + (KD + HG), HG)]])
            ahead()
            take_hidden((NF - 1) * HG, 0)
            take_hidden((NF - 1) * HG, 1)
            ffn_out(0)

            root()

            def features_of(dst, func):
                for half in range(2):
                    filled(half)
                    act.activation(dst[:, 2 * half:2 * half + 2, :],
                                   small[half][:, :].rearrange("p (a s) -> p a s", a=2), func).then_inc(small_free[half], 1)

            def decay(j):
                t.tick("level")
                act.wait_ge(arg_ready, t.value("level"))
                act.activation(dec[:, j % 2], dec[:, j % 2], ACT.Exp).then_inc(dec_ready, 1)

            def log_forget(k):
                if k == EVAC:
                    take(0, tok, ACT.Copy)
                if k == TURN + 4:
                    features_of(fT, ACT.Sigmoid)
                if k == TURN + 7:
                    t.tick("forget")
                    act.wait_ge(f_ready, t.value("forget"))
                    act.activation(dec[:, 1], dec[:, 0], ACT.Ln).then_inc(log_ready, 1)

            def output_squares():
                for tb in range(TB):
                    filled(tb)
                    act.activation(sq[:, tb], small[tb][:, :], ACT.Square).then_inc(osq_ready, 1)

            def output_root():
                t.tick("group")
                act.wait_ge(ovar_ready, t.value("group"))
                act.activation(hn[:, :, :], hn[:, :, :], ACT.Sqrt).then_inc(orstd_ready, 1)

            def group_work(k, every):
                if k == EVAC:
                    take(1, tok, ACT.Copy)
                if k == TURN + 2:
                    features_of(qT, ACT.Copy)
                if k == KD + EVAC:
                    take(0, vt, ACT.Copy)
                if k == 2 * KD + EVAC:
                    take(1, sg, ACT.Silu)
                for j in range(NL - 2):
                    if k == LEVEL_AT + every * j + 1:
                        decay(j)
                if k == O_AT + 2:
                    t.tick("small0", NL // 2)
                    t.tick("small1", NL // 2)
                    output_squares()
                if k == O_AT + 5:
                    output_root()
                log_forget(k - 3 * KD)

            chunk(KD, lambda k: features(k, gain, mod[:, 0, 0:KD]), True, AHEAD)
            chunk(KD, log_forget, True)
            with t.loop(act, NCH - 1, dict(PER_HGRN, used=4 * KD)):
                for part in range(4):
                    chunk(KD, lambda k: group_work(part * KD + k, EVERY), True)
            chunk(KD, lambda k: group_work(k, EVERY_LAST), True)
            chunk(KD, lambda k: group_work(KD + k, EVERY_LAST), True)
            for k in range(2 * KD, LEVEL_AT + EVERY_LAST * (NL - 3) + 2):
                for j in range(NL - 2):
                    if k == LEVEL_AT + EVERY_LAST * j + 1:
                        decay(j)
            ahead()
            take(1, sg, ACT.Silu)
            t.tick("small0", NL // 2)
            t.tick("small1", NL // 2)
            output_squares()
            output_root()
            for n in range(NCH):
                modulate(cols[:, C_HGAIN:C_HGAIN + KD], zero, n)
            with t.loop(act, NCH // 2, dict(PER_WOUT, used=2 * KD)) as i:
                def in_second(k):
                    if k == EVAC:
                        take_gate()
                    if k == EVAC + 4:
                        square_updated(i * 2)
                chunk(KD, None, False, AHEAD)
                chunk(KD, in_second)
                ahead()
                take_gate()
                square_updated(i * 2 + 1)
            root()
            ffn_pair(0, True, [])
            with t.loop(act, NF - 1, dict(PER_IN, used=2 * KD)) as i:
                ffn_pair(i * HG, False, [])
            ahead()
            take_hidden((NF - 1) * HG, 0)
            take_hidden((NF - 1) * HG, 1)
            ffn_out(1)
            root()

        @block.vector
        def _(dve):
            t = Tally()

            def lo(deep=False):
                r = t.get("step") // 2 % RAW
                wh, wl = split_slot(t, deep)
                dve.wait_ge(hi_ready, t.value("step", 1))
                dve.tensor_tensor(wl, raw[:, r, t.get("step") % 2], wh, ALU.subtract).then_inc(lo_ready, 1)
                t.tick("step")

            def ahead():
                for k in range(AHEAD):
                    lo()

            def chunk(n, after=None, deep=False, done=0, before=None):
                for k in range(n):
                    if before is not None:
                        before(k)
                    if k >= done:
                        lo(deep)
                    if after is not None:
                        after(k)
                t.tick("used", n)

            def fold(k):
                slot, buf, parts = t.get("ada") % ADA, unit_buffer(t), unit_parts(t)
                w, a = ada[:, slot, k % 2], accs[buf][:, k % parts]
                if k == 0 and t.some("unit", 2):
                    dve.wait_ge(unit_reduced, t.value("unit", -unit_lag(t)))
                if k % 2 == 0:
                    dve.wait_ge(ada_loaded[slot], t.value("ada", 1, 16, ADA))
                if k < parts:
                    ins = dve.tensor_scalar(a, w, cond[:, k:k + 1], None, ALU.mult)
                else:
                    if k % 2 == parts % 2:
                        dve.wait_ge(ada_half, t.value("ada", k % 2))
                    else:
                        dve.wait_ge(ada_used, t.value("ada"))
                    ins = dve.scalar_tensor_tensor(a, w, cond[:, k:k + 1], a, ALU.mult, ALU.add)
                ins.then_inc(ada_used if k % 2 else ada_half, 1)
                if k % 2:
                    t.tick("ada")
                if k == KD - 1:
                    dve.wait_ge(ada_half, t.value("ada"))
                    if parts == 1:
                        dve.wait_ge(ada_used, t.value("ada"))
                    dve.wait_ge(bias_loaded, t.value("unit", 1, 16))
                    a = accs[buf][0:1, 0]
                    dve.tensor_tensor(a, a, bias[:, :], ALU.add).then_inc(unit_summed, 1)
                    t.tick("unit")

            def unit():
                for k in range(KD):
                    fold(k)

            def norm_prepare(gains, branch):
                if gains is not None:
                    dve.wait_ge(unit_taken, t.value("unit"))
                    dve.scalar_tensor_tensor(gain[:, :], mod[:, branch, KD:2 * KD], 1.0, cols[:, gains:gains + KD],
                                             ALU.add, ALU.mult)
                dve.wait_ge(squared, t.value("sq"))
                dve.tensor_reduce(rstd[:, :], ssq[:, :, :], AXX, ALU.add).then_inc(var_step, 1)
                t.tick("var")
                dve.wait_ge(var_step, t.value("var"))
                dve.tensor_scalar(rstd[:, :], rstd[:, :], 1.0 / D, EPS, ALU.mult, ALU.add).then_inc(var_step, 1)
                t.tick("var")
                dve.wait_ge(var_step, t.value("var"))
                dve.reciprocal(rstd[:, :], rstd[:, :]).then_inc(var_ready, 1)
                t.tick("norm")
                dve.wait_ge(rstd_ready, t.value("norm"))

            def normalise(n):
                if t.some("small1"):
                    dve.wait_ge(small_full[1], t.value("small1"))
                if t.some("upd"):
                    dve.wait_ge(x_updated, t.value("upd"))
                for tb in range(TB):
                    ins = dve.tensor_scalar(tok[:, tb], xs[:, tb, n * CH:(n + 1) * CH], rstd[:, tb:tb + 1], None, ALU.mult)
                ins.then_inc(tok_ready, 1)

            def split_h(src, k, n):
                dve.tensor_copy(h_hi[:, k:k + n], src).then_inc(h_high, 1)
                t.tick("hh")
                dve.wait_ge(h_high, t.value("hh"))
                return dve.tensor_tensor(h_lo[:, k:k + n], src, h_hi[:, k:k + n], ALU.subtract)

            def split_feat(n):
                for half in range(2):
                    t.tick(f"small{half}")
                    dve.wait_ge(small_free[half], t.value(f"small{half}"))
                    split_h(feat[:, half], n * HG + 2 * half, 2).then_inc(h_ready, 1)

            def normalise_ahead(n):
                t.n["small1"] += 1
                normalise(n)
                t.n["small1"] -= 1

            def features(k):
                if k == 0:
                    normalise(0)
                    for n in range(2):
                        normalise_ahead(n + 1)
                        split_feat(n)
                if k % HG == 0 and k // HG >= 2:
                    if k // HG + 1 < NCH:
                        normalise_ahead(k // HG + 1)
                    split_feat(k // HG)

            def update(par, at, gates=gate, later=0):
                dve.wait_ge(w_used, t.value("used"))
                dve.wait_ge(unit_taken, t.value("unit", -later))
                if t.some("upd"):
                    dve.wait_ge(x_updated, t.value("upd"))
                t.tick("upd")
                term = gates[:, :].unsqueeze(1).to_broadcast([P, TB, CH])
                dve.tensor_tensor(tok[:, :, :], prod[par][:, :, :], term, ALU.mult).then_inc(prod_free[par], 1)
                dve.wait_ge(prod_free[par], t.value("prod", 1, 1, 2))
                xc = xs[:, :, bass.ds(at * CH, CH)]
                dve.tensor_tensor(xc, xc, tok[:, :, :], ALU.add).then_inc(x_updated, 1)

            dve.wait_ge(small_full[0], 1)
            dve.tensor_copy(cols[:, :], small[0][:, 0:P]).then_inc(small_free[0], 1)
            t.tick("small0")
            dve.wait_ge(small_free[0], 1)
            lb = cols[:, C_LB:C_LB + 2 * KD].rearrange("p (l k) -> p l k", l=2)
            dve.tensor_copy(lbt[:, 2:4], lb).then_inc(cols_ready, 1)
            dve.tensor_tensor(lbt[:, 0], lb[:, 0], lb[:, 1], ALU.max).then_inc(lb_max, 1)
            dve.wait_ge(lb_max, 1)
            dve.wait_ge(cols_ready, 1)
            for l in range(2):
                dve.tensor_tensor(lbt[:, 2 + l], lbt[:, 2 + l], lbt[:, 0], ALU.subtract).then_inc(lb_max, 1)
            dve.wait_ge(lb_exp, 1)
            dve.tensor_tensor(lbt[:, 0], lbt[:, 2], lbt[:, 3], ALU.add).then_inc(lb_ready, 1)
            dve.wait_ge(lb_ready, 1)
            dve.reciprocal(lbt[:, 1], lbt[:, 0]).then_inc(lb_ready, 1)
            dve.wait_ge(lb_ready, 2)
            for l in range(2):
                dve.tensor_tensor(lbt[:, 2 + l], lbt[:, 2 + l], lbt[:, 1], ALU.mult).then_inc(lb_ready, 1)
            dve.wait_ge(lb_ready, 4)
            dve.tensor_tensor(lbt[:, 0], lbt[:, 2], lbt[:, 3], ALU.add).then_inc(lb_ready, 1)
            dve.wait_ge(lb_ready, 5)
            dve.tensor_tensor(lower[:, :], lbt[:, 0], lbt[:, 2], ALU.subtract).then_inc(lb_ready, 1)
            dve.wait_ge(lb_ready, 6)
            dve.tensor_scalar(upper[:, :], lower[:, :], -1.0, 1.0, ALU.mult, ALU.add).then_inc(lb_ready, 1)
            dve.wait_ge(cond_ready, 1)
            t.tick("sq", NCH * TB)
            unit()
            unit()
            with t.loop(dve, NCH - 1, PER_2UNITS):
                unit()
                unit()

            def pool_group(n, w):
                src, span, lo_end = padded, 1, 1
                step = [t.get("pool")]

                def done(ins):
                    ins.then_inc(pool_step, 1)
                    t.tick("pool")
                    dve.wait_ge(pool_step, t.value("pool"))

                while span < w:
                    dst = win[0] if src is not win[0] else win[1]
                    done(dve.tensor_tensor(dst[:, :, lo_end:], src[:, :, lo_end:],
                                           src[:, :, lo_end - span:PAD + S - span], ALU.add))
                    src, span = dst, 2 * span
                    lo_end += span
                h = padded[:, :, PAD:]
                done(dve.scalar_tensor_tensor(diff[:, :, :], src[:, :, PAD:], 1.0 / w, h, ALU.mult, ALU.subtract))
                done(dve.tensor_tensor(edge[:, :, 0:w], src[:, :, PAD:PAD + w],
                                       inv[:, 0:w].unsqueeze(1).to_broadcast([P, HG, w]), ALU.mult))
                done(dve.tensor_tensor(diff[:, :, 0:w], edge[:, :, 0:w], h[:, :, 0:w], ALU.subtract))
                split_h(diff[:, :, :], n * HG, HG).then_inc(h_ready, 2)

            norm_prepare(C_GMIX, 0)
            def pool_update(n):
                dve.wait_ge(pscale_loaded, 16 * (n + 1))
                dve.wait_ge(unit_taken, t.value("unit"))
                dve.tensor_tensor(pscale[:, :], pscale[:, :], gate[:, :], ALU.mult).then_inc(pscale_ready, 1)
                dve.wait_ge(pscale_ready, n + 1)
                dve.wait_ge(small_full[1], t.value("small1"))
                update(n % 2, n, pscale)
                t.tick("prod")
                t.tick("sq", TB)

            dve.wait_ge(consts, N_CONSTS)
            for n, w in enumerate(WINDOWS):
                normalise(n)
                for k in range(KD // 2):
                    fold(k)
                t.tick("small0")
                t.tick("small1")
                if n:
                    pool_update(n - 1)
                dve.wait_ge(small_free[0], t.value("small0"))
                dve.wait_ge(small_free[1], t.value("small1"))
                pool_group(n, w)
                chunk(HG)
                for k in range(KD // 2, KD):
                    fold(k)
            pool_update(NCH - 1)
            with t.loop(dve, NCH, PER_2UNITS):
                unit()
                unit()

            def take_value():
                dve.wait_ge(w_used, t.value("used"))
                dve.wait_ge(prod_free[0], t.value("prod", 0, 1, 2))
                dve.tensor_tensor(tok[:, :, :], tok[:, :, :], prod[1][:, :, :], ALU.mult).then_inc(prod_free[1], 1)

            def low_hidden(at, half):
                t.tick(f"small{half}")
                t.tick("hid")
                dve.wait_ge(ghi_ready, t.value("hid"))
                blocks = bass.ds(at + 2 * half, 2)
                dve.tensor_tensor(g_lo[:, blocks, :], small[half][:, :].rearrange("p (a s) -> p a s", a=2),
                                  g_hi[:, blocks, :], ALU.subtract).then_inc(small_free[half], 1)

            def ffn_pair(at, first, units):
                def in_gate(k):
                    if k == EVAC - 1 and not first:
                        take_value()
                    for span in units:
                        for b in due(k, KD, *span):
                            fold(b)
                    if k == TURN + 3 and not first:
                        low_hidden(at, 0)
                    if k == TURN + 4 and not first:
                        low_hidden(at, 1)

                def in_value(k):
                    for span in units:
                        for b in due(k + KD, KD, *span):
                            fold(b)

                chunk(KD, in_gate, False, AHEAD if first else 0, features if first else None)
                chunk(KD, in_value)
                t.tick("prod", 2)

            def ffn_out(layer):
                spans = OUT_UNITS[2 - layer]
                def pair(i, end):
                    for o in range(2):
                        def in_out(k):
                            if k == EVAC + 1 and o == 1:
                                update(0, i * 2, gate, len(spans) - 1)
                            for span in spans:
                                for b in due(k, KD, *span):
                                    fold(b)
                        chunk(KF, in_out, False, AHEAD if o == 0 else 0)
                    if not end:
                        ahead()
                    update(1, i * 2 + 1, gate, len(spans) - 1)
                    t.tick("prod", 2)
                    t.tick("sq", 2 * TB)

                with t.loop(dve, NCH // 2 - layer, dict(PER_OUT[2 - layer], used=2 * KF)) as i:
                    pair(i, False)
                if layer:
                    pair(NCH // 2 - 1, True)

            ahead()
            norm_prepare(C_GFFN, 1)
            ffn_pair(0, True, FIRST_UNITS)
            with t.loop(dve, 2 * NCH - 1, dict(PER_IN_UNIT, used=2 * KD)) as i:
                ffn_pair(i * HG, False, [IN_UNIT])
            with t.loop(dve, NF - 2 * NCH, dict(PER_IN_UNIT, used=2 * KD)) as i:
                ffn_pair(i * HG + (2 * NCH - 1) * HG, False, [IN_UNIT])
            ahead()
            take_value()
            low_hidden((NF - 1) * HG, 0)
            low_hidden((NF - 1) * HG, 1)
            ffn_out(0)

            norm_prepare(C_GMIX + KD, 0)
            dve.wait_ge(hgrn_consts, N_HGRN_CONSTS)
            b4 = lambda a, h: a.rearrange("p a s -> p (a s)").rearrange("p (n two h) -> p n two h", two=2, h=h)

            def forget(i):
                for half in range(2):
                    t.tick(f"small{half}")
                    dve.wait_ge(small_free[half], t.value(f"small{half}"))
                for hd in range(HG):
                    ins = dve.tensor_scalar(fT[:, hd], fT[:, hd], upper[:, bass.ds(i * HG + hd, 1)],
                                            lower[:, bass.ds(i * HG + hd, 1)], ALU.mult, ALU.add)
                ins.then_inc(fT_ready, 1)
                t.tick("bs")
                dve.wait_ge(fT_ready, t.value("bs"))
                dve.tensor_scalar(kT[:, :, :], fT[:, :, :], -1.0, 1.0, ALU.mult, ALU.add)
                dve.tensor_scalar(dec[:, 0], fT[:, :, :], LN_FLOOR, None, ALU.max).then_inc(f_ready, 1)

            def cumulate():
                t.tick("logs")
                dve.wait_ge(log_ready, t.value("logs"))
                dve.tensor_tensor_scan(bT[:, :, :].rearrange("p a s -> p (a s)"), keep[:, :],
                                       dec[:, 1].rearrange("p a s -> p (a s)"), 0.0, ALU.mult, ALU.add).then_inc(b_ready, 1)

            def exponents(j):
                d = dec[:, j % 2]
                if j == 0:
                    dve.wait_ge(b_ready, t.value("group", 1))
                    ref = bT[:, :, P - 1:P].to_broadcast([P, HG, P])
                    dve.tensor_tensor(d[:, :, 0:P], ref, bT[:, :, 0:P], ALU.subtract)
                    dve.tensor_copy(d[:, :, P:], bT[:, :, P:]).then_inc(arg_ready, 1)
                    return
                h = LEVELS[j - 1]
                b, e = b4(bT[:, :, :], h), b4(d, h)
                ref = b[:, :, 0, h - 1:h].to_broadcast([P, HG * S // (2 * h), h])
                dve.tensor_tensor(e[:, :, 0], ref, b[:, :, 0], ALU.subtract)
                dve.tensor_tensor(e[:, :, 1], b[:, :, 1], ref, ALU.subtract).then_inc(arg_ready, 1)

            def decayed(j):
                t.tick("level")
                dve.wait_ge(dec_ready, t.value("level"))
                d, kd, qd = dec[:, j % 2], kdec[:, j % 2], qdec[:, j % 2]
                if j == 0:
                    dve.tensor_tensor(kd[:, :, 0:P], kT[:, :, 0:P], d[:, :, 0:P], ALU.mult)
                    dve.tensor_tensor(qd, qT[:, :, P:], d[:, :, P:], ALU.mult).then_inc(qk_ready, 1)
                    return
                h = LEVELS[j - 1]
                dve.tensor_tensor(b4(kd, h)[:, :, 0], b4(kT[:, :, :], h)[:, :, 0], b4(d, h)[:, :, 0], ALU.mult)
                dve.tensor_tensor(qd.rearrange("p a s -> p (a s)").rearrange("p (n h) -> p n h", h=h),
                                  b4(qT[:, :, :], h)[:, :, 1], b4(d, h)[:, :, 1], ALU.mult).then_inc(qk_ready, 1)

            def scores(k):
                bk = k % 2
                t.tick(f"small{bk}")
                dve.wait_ge(small_full[bk], t.value(f"small{bk}"))
                if k < 2:
                    dve.tensor_tensor(sdiag[:, 2 * k:2 * k + 2].rearrange("p a b s -> p (a b) s"),
                                      small[bk][:, :].rearrange("p (n s) -> p n s", s=P),
                                      ident[:, :].unsqueeze(1).to_broadcast([P, 2 * TB, P]), ALU.mult).then_inc(small_free[bk], 1)
                    return
                if k == 2:
                    dve.tensor_copy(scross[:, :, :].rearrange("p a s -> p (a s)"), small[bk][:, :]).then_inc(small_free[bk], 1)
                    return
                h = LEVELS[k - 3]
                m = masks[:, k - 3, :].unsqueeze(1).to_broadcast([P, HG * TB, P // 2])
                if k > 3:
                    dve.wait_ge(s_masked, t.value("sm"))
                dve.tensor_tensor(smask[:, :, :], small[bk][:, :].rearrange("p (n s) -> p n s", s=P // 2), m,
                                  ALU.mult).then_inc(small_free[bk], 1)
                dve.wait_ge(small_free[bk], t.value(f"small{bk}"))
                if k == 3:
                    dve.wait_ge(small_free[1], t.value("small1", -1))
                target = b4(sdiag[:, :, :, :].rearrange("p a b s -> p (a b) s"), h)[:, :, 1]
                dve.tensor_tensor(target, target, smask[:, :, :].rearrange("p n s -> p (n s)").rearrange("p (n h) -> p n h", h=h),
                                  ALU.add).then_inc(s_ready if k == NL - 1 else s_masked, 1)
                if k < NL - 1:
                    t.tick("sm")

            def output_norm():
                for tb in range(TB):
                    t.tick(f"small{tb}")
                t.tick("group")
                dve.wait_ge(osq_ready, t.value("group", 0, TB))
                dve.tensor_reduce(hn[:, :, :].rearrange("p a b -> p (a b)"),
                                  sq.rearrange("p a (b s) -> p (a b) s", s=P), AXX, ALU.add).then_inc(ovar_step, 1)
                t.tick("ov")
                dve.wait_ge(ovar_step, t.value("ov"))
                dve.tensor_scalar(hn[:, :, :], hn[:, :, :], 1.0 / P, EPS, ALU.mult, ALU.add).then_inc(ovar_step, 1)
                t.tick("ov")
                dve.wait_ge(ovar_step, t.value("ov"))
                dve.reciprocal(hn[:, :, :], hn[:, :, :]).then_inc(ovar_ready, 1)

            def output_gate(i):
                dve.wait_ge(orstd_ready, t.value("group"))
                for tb in range(TB):
                    o = og[:, tb, bass.ds(i * CH, CH)].rearrange("p (b s) -> p b s", s=P)
                    dve.tensor_tensor(o, small[tb][:, :].rearrange("p (b s) -> p b s", s=P),
                                      hn[:, tb].unsqueeze(2).to_broadcast([P, HG, P]), ALU.mult).then_inc(small_free[tb], 1)
                for tb in range(TB):
                    dve.wait_ge(small_free[tb], t.value(f"small{tb}"))
                dve.wait_ge(prod_free[1], t.value("prod", 1, 1, 2))
                o = og[:, :, bass.ds(i * CH, CH)]
                dve.tensor_tensor(o, o, sg[:, :, :], ALU.mult).then_inc(og_ready, 1)

            def forget_work(k, i):
                if k == TURN + 5:
                    forget(i)
                if k == KD - 1:
                    cumulate()

            def group_work(k, i, every):
                for j in range(NL - 2):
                    at = LEVEL_AT + every * j
                    if k == at:
                        exponents(j)
                    if k == at + 2:
                        decayed(j)
                if k == LEVEL_AT + 1:
                    for half in range(2):
                        t.tick(f"small{half}")
                        dve.wait_ge(small_free[half], t.value(f"small{half}"))
                if k in (LEVEL_AT + 3, LEVEL_AT + 4):
                    scores(k - LEVEL_AT - 3)
                for j in range(NL - 2):
                    if k == LEVEL_AT + every * j + 5:
                        scores(2 + j)
                if k == O_AT + 3:
                    output_norm()
                if k == O_AT + 5:
                    output_gate(i)
                forget_work(k - 3 * KD, i + 1)

            chunk(KD, None, True, AHEAD, features)
            chunk(KD, lambda k: forget_work(k, 0), True)
            t.tick("prod", 2)
            with t.loop(dve, NCH - 1, dict(PER_HGRN, used=4 * KD, bs=1, logs=1, sm=NL - 4, ov=2)) as i:
                for part in range(4):
                    chunk(KD, lambda k: group_work(part * KD + k, i, EVERY), True)
                t.tick("prod", 4)
            chunk(KD, lambda k: group_work(k, NCH - 1, EVERY_LAST), True)
            chunk(KD, lambda k: group_work(KD + k, NCH - 1, EVERY_LAST), True)
            for k in range(2 * KD, LEVEL_AT + EVERY_LAST * (NL - 3) + 6):
                group_work(k, NCH - 1, EVERY_LAST)
            ahead()
            output_norm()
            output_gate(NCH - 1)
            t.tick("prod", 2)
            for n in range(NCH):
                split_feat(n)
            with t.loop(dve, NCH // 2, dict(PER_WOUT, used=2 * KD)) as i:
                def in_wout(k):
                    for b in due(k, KD, *WOUT_UNIT):
                        fold(b)

                def in_second(k):
                    if k == EVAC + 2:
                        update(0, i * 2)
                    in_wout(k)

                chunk(KD, in_wout, False, AHEAD)
                chunk(KD, in_second)
                ahead()
                update(1, i * 2 + 1)
                t.tick("prod", 2)
                t.tick("sq", 2 * TB)
            norm_prepare(C_GFFN + KD, 1)
            ffn_pair(0, True, [])
            with t.loop(dve, NF - 1, dict(PER_IN, used=2 * KD)) as i:
                ffn_pair(i * HG, False, [])
            ahead()
            take_value()
            low_hidden((NF - 1) * HG, 0)
            low_hidden((NF - 1) * HG, 1)
            ffn_out(1)
            norm_prepare(None, 0)
            dve.wait_ge(fgain_loaded, 16)
            for tb in range(TB):
                dve.scalar_tensor_tensor(xs[:, tb], xs[:, tb], rstd[:, tb:tb + 1], fgain, ALU.mult, ALU.mult).then_inc(y_ready, 1)


_NAMES = ["x", "c", "norm_mix_gain", "norm_ffn_gain", "w_ada", "b_ada", "pool_w", "pool_scale", "hgrn_w_in",
          "hgrn_w_out", "hgrn_norm_gain", "hgrn_lb", "w_ffn_in", "w_ffn_out", "final_gain"]


def kernel(**inputs):
    import concourse.bacc as bacc
    from concourse.bass_utils import run_bass_kernel_spmd

    nc = bacc.Bacc("TRN2", target_bir_lowering=False, num_devices=1)
    arrays, args = {}, []
    for name in _NAMES:
        a = np.ascontiguousarray(inputs[name])
        arrays[f"in_{name}"] = a
        args.append(nc.dram_tensor(f"in_{name}", a.shape, mybir.dt.from_np(a.dtype), kind="ExternalInput").ap())
    out = nc.dram_tensor("out", inputs["x"].shape, F32, kind="ExternalOutput").ap()
    build(nc, *args, out)
    result = run_bass_kernel_spmd(nc, [arrays], core_ids=[0])
    return result.results[0]["out"]
```

```python
from contextlib import ExitStack, contextmanager

import numpy as np
import concourse.bass as bass
from concourse import mybir

F32 = mybir.dt.float32
F32R = mybir.dt.float32r
BF16 = mybir.dt.bfloat16
ALU = mybir.AluOpType
ACT = mybir.ActivationFunctionType
AXX = mybir.AxisListType.X

P = 128
CH = 512
EPS = 1e-6
WINDOWS = (2, 4, 8, 16)
PAD = 16
LEVELS = (64, 32, 16, 8, 4, 2, 1)
LN_FLOOR = 2.0 ** -60


class Tally:

    def __init__(self):
        self.n = {}
        self.i = None
        self.first = 0
        self.per = {}

    def some(self, name, n=1):
        return self.get(name) >= n

    def get(self, name):
        return self.n.get(name, 0)

    def tick(self, name, k=1):
        self.n[name] = self.get(name) + k

    def value(self, name, add=0, scale=1, div=1):
        const = scale * (self.get(name) // div + add)
        if self.i is None or not self.per.get(name, 0):
            return const
        assert self.per[name] % div == 0
        step = scale * self.per[name] // div
        return self.i * step + (const - self.first * step)

    @contextmanager
    def loop(self, eng, count, per, first=0):
        before = dict(self.n)
        with eng.Fori(first, first + count) as i:
            self.i, self.first, self.per = i, first, per
            yield i
        for name in list(self.n):
            grown = self.get(name) - before.get(name, 0)
            assert grown in (0, per.get(name, 0)), (name, grown, per.get(name, 0))
            self.n[name] = before.get(name, 0) + count * grown
        self.i, self.per = None, {}


def due(step, n, first, last):
    return [k for k in range(n) if first + k * (last - first + 1) // n == step]


def build(nc, x, c, norm_mix_gain, norm_ffn_gain, w_ada, b_ada, pool_w, pool_scale, hgrn_w_in,
          hgrn_w_out, hgrn_norm_gain, hgrn_lb, w_ffn_in, w_ffn_out, final_gain, out):
    D = x.shape[2]
    TB = x.shape[1] // P
    S = TB * P
    KD = D // P
    NCH = D // CH
    F = w_ffn_out.shape[1]
    KF = F // P
    NF = F // CH
    HG = CH // P
    KU = KD // 2
    NL = 3 + len(LEVELS)
    RAW = 4
    SPL = 4
    ADA = 4
    PE_LOADS = [6] * (NCH - 1) + [KU - ADA]
    AHEAD = SPL
    assert AHEAD == HG

    EVAC = 3
    TURN = 6
    IN_UNIT = (0, 24)
    OUT_UNITS = {1: [(0, 31)], 2: [(0, 15), (20, 35)]}
    WOUT_UNIT = (4, 15)
    HGRN_UNIT = (0, 52)
    SUM = 2
    LEVEL_AT, EVERY, EVERY_LAST, O_AT = 8, 5, 3, 3 * KD + 3

    def per(steps, chunks, units=0, **more):
        return dict(step=steps, raw=steps // 2, prod=chunks, unit=units, ada=KU * units, folded=KU * units, **more)

    PER_2UNITS = dict(unit=2, ada=2 * KU, folded=2 * KU)
    PER_IN = per(2 * KD, 2, 0, small0=1, small1=1, hid=2)
    PER_IN_UNIT = per(2 * KD, 2, 1, small0=1, small1=1, hid=2)
    PER_OUT = {n: per(2 * KF, 2, 2 * n, upd=2, sq=2 * TB) for n in (1, 2)}
    PER_WOUT = per(2 * KD, 2, 2, upd=2, sq=2 * TB)
    PER_HGRN = per(4 * KD, 4, 1, small0=3 + NL // 2, small1=3 + NL // 2, level=NL - 2, group=1, forget=1)

    CLOSE = 5 * NCH

    def unit_buffer(t):
        return t.get("unit") % 2 if t.get("unit") < CLOSE else 0

    def unit_parts(t):
        return 2 if t.get("unit") < CLOSE else 1

    def unit_lag(t):
        return 1 if t.get("unit") < CLOSE else 0

    ctx = ExitStack()
    with ctx:
        def sb(name, shape, dt=F32, where=ctx):
            return where.enter_context(nc.sbuf_tensor(name, shape, dt))

        def sem(name):
            return ctx.enter_context(nc.semaphore(name))

        xs = sb("xs", [P, TB, D])
        h_hi = sb("h_hi", [P, KD, S], F32R)
        h_lo = sb("h_lo", [P, KD, S], F32R)
        raw = sb("raw", [P, RAW, 2, CH])
        w_hi = sb("w_hi", [P, SPL, CH], F32R)
        w_lo = sb("w_lo", [P, SPL, CH], F32R)
        ada = sb("ada", [P, ADA, 2, CH])
        acc = sb("acc", [P, 2, CH])
        bias = sb("bias", [1, CH])
        gate = sb("gate", [P, CH])
        tok = sb("tok", [P, TB, CH])
        feat = sb("feat", [P, 2, 2, S])
        junk = sb("junk", [P, CH], BF16)
        ident = sb("ident", [P, P])
        ones = sb("ones", [P, P])
        cols = sb("cols", [P, P])
        cond = sb("cond", [P, KD])
        mod = sb("mod", [P, 2, 2 * KD])
        gain = sb("gain", [P, KD])
        zero = sb("zero", [P, KD])
        lower = sb("lower", [P, KD])
        upper = sb("upper", [P, KD])
        ssq = sb("ssq", [P, TB, NCH])
        rstd = sb("rstd", [P, TB])
        spare = sb("spare", [P, 1])

        with ExitStack() as pooling:
            rows = sb("rows", [P, P], where=pooling)
            pscale = sb("pscale", [P, NCH, CH], where=pooling)
            cond_rows = sb("cond_rows", [P, 2 * max(PE_LOADS), P], where=pooling)
            padded = sb("padded", [P, HG, PAD + S], where=pooling)
            win = [sb(f"win{i}", [P, HG, PAD + S], where=pooling) for i in range(2)]
            diff = sb("diff", [P, HG, S], where=pooling)
            edge = sb("edge", [P, HG, PAD], where=pooling)
            inv = sb("inv", [P, PAD], where=pooling)
            lbt = sb("lbt", [P, 4, KD], where=pooling)
        with ExitStack() as hgrn:
            keep = sb("keep", [P, HG * S], BF16, where=hgrn)
            masks = sb("masks", [P, len(LEVELS), P // 2], where=hgrn)
            fT = sb("fT", [P, HG, S], where=hgrn)
            kT = sb("kT", [P, HG, S], where=hgrn)
            bT = sb("bT", [P, HG, S], where=hgrn)
            qT = sb("qT", [P, HG, S], where=hgrn)
            dec = sb("dec", [P, 2, HG, S], where=hgrn)
            kdec = sb("kdec", [P, 2, HG, S], where=hgrn)
            qdec = sb("qdec", [P, 2, HG, P], where=hgrn)
            sdiag = sb("sdiag", [P, HG, TB, P], where=hgrn)
            scross = sb("scross", [P, HG, P], where=hgrn)
            smask = sb("smask", [P, HG * TB, P // 2], where=hgrn)
            vt = sb("vt", [P, TB, CH], where=hgrn)
            sg = sb("sg", [P, TB, CH], where=hgrn)
            hn = sb("hn", [P, TB, HG], where=hgrn)
            og = sb("og", [P, TB, D], where=hgrn)
            w_hi2 = sb("w_hi2", [P, SPL, CH], F32R, where=hgrn)
            w_lo2 = sb("w_lo2", [P, SPL, CH], F32R, where=hgrn)
        g_hi = sb("g_hi", [P, KF, S], F32R)
        g_lo = sb("g_lo", [P, KF, S], F32R)
        sq = fT[:, :, :].rearrange("p a s -> p (a s)").rearrange("p (t n) -> p t n", t=TB)
        accs = [acc, feat[:, :, :, :].rearrange("p a b s -> p a (b s)")]
        fgain = ada[:, 0:2].rearrange("p a b n -> p (a b n)")

        prod = [ctx.enter_context(nc.psum_tensor(f"prod{i}", [P, TB, CH], F32)) for i in range(2)]
        small = [ctx.enter_context(nc.psum_tensor(f"small{i}", [P, CH], F32)) for i in range(2)]
        modp = ctx.enter_context(nc.psum_tensor("modp", [P, CH], F32))

        C_GMIX, C_GFFN, C_HGAIN, C_LB = KD, 3 * KD, 5 * KD, 6 * KD

        raw_loaded = [sem(f"raw_loaded{i}") for i in range(RAW)]
        ada_loaded = [sem(f"ada_loaded{i}") for i in range(ADA)]
        params_loaded = sem("params_loaded")
        x_loaded = sem("x_loaded")
        bias_loaded = sem("bias_loaded")
        pscale_loaded = sem("pscale_loaded")
        pe_used = sem("pe_used")
        rows_ready = sem("rows_ready")
        fgain_loaded = sem("fgain_loaded")
        stored = sem("stored")
        consts = sem("consts")
        hgrn_consts = sem("hgrn_consts")
        w_used = sem("w_used")
        unit_reduced = sem("unit_reduced")
        small_full = [sem(f"small_full{i}") for i in range(2)]
        hi_ready = sem("hi_ready")
        unit_taken = sem("unit_taken")
        cond_ready = sem("cond_ready")
        lb_exp = sem("lb_exp")
        squared = sem("squared")
        rstd_ready = sem("rstd_ready")
        table_ready = sem("table_ready")
        ghi_ready = sem("ghi_ready")
        log_ready = sem("log_ready")
        dec_ready = sem("dec_ready")
        osq_ready = sem("osq_ready")
        orstd_ready = sem("orstd_ready")
        lo_ready = sem("lo_ready")
        ada_half = sem("ada_half")
        ada_used = sem("ada_used")
        unit_summed = sem("unit_summed")
        cols_ready = sem("cols_ready")
        lb_max = sem("lb_max")
        lb_ready = sem("lb_ready")
        var_step = sem("var_step")
        var_ready = sem("var_ready")
        tok_ready = sem("tok_ready")
        h_high = sem("h_high")
        h_ready = sem("h_ready")
        pool_step = sem("pool_step")
        pscale_ready = sem("pscale_ready")
        x_updated = sem("x_updated")
        f_ready = sem("f_ready")
        fT_ready = sem("fT_ready")
        b_ready = sem("b_ready")
        arg_ready = sem("arg_ready")
        qk_ready = sem("qk_ready")
        s_masked = sem("s_masked")
        s_ready = sem("s_ready")
        ovar_step = sem("ovar_step")
        ovar_ready = sem("ovar_ready")
        og_ready = sem("og_ready")
        final_step = sem("final_step")
        y_ready = sem("y_ready")
        prod_free = [sem(f"prod_free{i}") for i in range(2)]
        small_free = [sem(f"small_free{i}") for i in range(2)]

        def split_slot(t, deep):
            k = t.get("step") % (2 * SPL if deep else SPL)
            return (w_hi[:, k], w_lo[:, k]) if k < SPL else (w_hi2[:, k - SPL], w_lo2[:, k - SPL])

        block = ctx.enter_context(nc.Block())
        FFN_STEPS = 2 * KD * NF + KF * NCH

        @block.sync
        def _(sp):
            t = Tally()

            def load_w(src):
                slot = t.get("raw") % RAW
                if t.some("raw", RAW):
                    sp.wait_ge(lo_ready, t.value("raw", 1 - RAW, 2))
                sp.dma_start(raw[:, slot], src.rearrange("(a p) n -> p a n", p=P)).then_inc(raw_loaded[slot], 16)
                t.tick("raw")

            def load_ada(layer, at, k):
                if k == ADA:
                    if t.some("unit"):
                        sp.wait_ge(unit_summed, t.value("unit"))
                    sp.dma_start(bias[:, :], b_ada[layer:layer + 1, bass.ds(at, CH)]).then_inc(bias_loaded, 16)
                slot = t.get("ada") % ADA
                n = t.get("unit") - 2 * NCH
                ours = PE_LOADS[n] if 0 <= n < NCH else 0
                last = PE_LOADS[n - 1] if 0 < n < NCH else 0
                if k < ours:
                    if k + KU - ADA < last:
                        sp.wait_ge(pe_used, t.get("multiplied") + k + KU - ADA - last + 1)
                    elif k < ADA:
                        sp.wait_ge(ada_used, t.get("folded") + k + 1 - ADA)
                    else:
                        sp.wait_ge(pe_used, t.get("multiplied") + k + 1 - ADA)
                elif ours:
                    sp.wait_ge(pe_used, t.get("multiplied") + k + 1 - ADA)
                elif t.some("ada", ADA):
                    sp.wait_ge(ada_used, t.value("folded", 1 - ADA))
                src = w_ada[layer, 2 * k * P:2 * (k + 1) * P, bass.ds(at, CH)]
                sp.dma_start(ada[:, slot], src.rearrange("(a p) n -> p a n", p=P)).then_inc(ada_loaded[slot], 16)
                t.tick("ada")
                if k >= ours:
                    t.tick("folded")
                if k == KU - 1:
                    t.tick("multiplied", ours)
                    t.tick("unit")

            def load_unit(layer, at):
                for k in range(KU):
                    load_ada(layer, at, k)

            def load_chunk(src, at, blocks, units=(), shift=0, loaded=0):
                for s in range(blocks):
                    if s % 2 == 0 and s >= loaded:
                        load_w(src[s * P:(s + 2) * P, bass.ds(at, CH)])
                    for layer, col, span in units:
                        for k in due(s + shift, KU, *span):
                            load_ada(layer, col, k)

            at = 0
            for src in (c, norm_mix_gain, norm_ffn_gain, hgrn_norm_gain, hgrn_lb):
                n = src.shape[0] * KD
                sp.dma_start(rows[at:at + n, :], src.rearrange("l (k p) -> (l k) p", p=P)).then_inc(params_loaded, 16)
                at += n
            load_unit(0, 0)
            for tb in range(TB):
                sp.dma_start(xs[:, tb], x[0, tb * P:(tb + 1) * P, :]).then_inc(x_loaded, 16)
            load_unit(0, CH)
            with t.loop(sp, NCH - 1, PER_2UNITS) as i:
                load_unit(0, i * 2 * CH + 2 * CH)
                load_unit(0, i * 2 * CH + 3 * CH)
            for n in range(NCH):
                load_chunk(pool_w[0, n], 0, HG)
                load_unit(0, 2 * D + n * CH)
                if n == 0:
                    sp.dma_start(pscale[:, :, :].rearrange("p a n -> p (a n)"),
                                 pool_scale[0:1, :].to_broadcast([P, D])).then_inc(pscale_loaded, 16)
            load_chunk(w_ffn_in[0], 0, AHEAD)
            with t.loop(sp, NCH, PER_2UNITS) as i:
                load_unit(0, i * 2 * CH + 3 * D)
                load_unit(0, i * 2 * CH + (3 * D + CH))

            def load_pair(at, units, loaded=0):
                load_chunk(w_ffn_in[0 if units is not None else 1], at, KD, units or (), 0, loaded)
                load_chunk(w_ffn_in[0 if units is not None else 1], at + F, KD, units or (), KD)

            def load_ffn_out(layer):
                with t.loop(sp, NCH // 2, PER_OUT[2 - layer]) as i:
                    for o in range(2):
                        units = [(layer, i * 2 * CH + (5 * D + o * CH)), (1, i * 2 * CH + (3 * D + o * CH))]
                        load_chunk(w_ffn_out[layer], i * 2 * CH + o * CH, KF,
                                   [(*unit, span) for unit, span in zip(units, OUT_UNITS[2 - layer])])

            load_pair(0, [], AHEAD)
            with t.loop(sp, 2 * NCH, PER_IN_UNIT) as i:
                load_pair(i * CH + CH, [(1, i * CH, IN_UNIT)])
            load_pair((2 * NCH + 1) * CH, [(1, 4 * D, IN_UNIT)])
            with t.loop(sp, NF - 2 * NCH - 2, PER_IN) as i:
                load_pair(i * CH + (2 * NCH + 2) * CH, [])
            load_ffn_out(0)
            load_chunk(hgrn_w_in[0], D, KD)
            load_chunk(hgrn_w_in[0], 0, KD)
            with t.loop(sp, NCH - 1, PER_HGRN) as i:
                unit = [(1, i * CH + (4 * D + CH), HGRN_UNIT)]
                load_chunk(hgrn_w_in[0], i * CH + 2 * D, KD, unit)
                load_chunk(hgrn_w_in[0], i * CH + 3 * D, KD, unit, KD)
                load_chunk(hgrn_w_in[0], i * CH + (D + CH), KD, unit, 2 * KD)
                load_chunk(hgrn_w_in[0], i * CH + CH, KD, unit, 3 * KD)
            load_chunk(hgrn_w_in[0], 2 * D + (NCH - 1) * CH, KD)
            load_chunk(hgrn_w_in[0], 3 * D + (NCH - 1) * CH, KD)
            with t.loop(sp, NCH // 2, PER_WOUT) as i:
                for o in range(2):
                    load_chunk(hgrn_w_out[0], i * 2 * CH + o * CH, KD,
                               [(1, i * 2 * CH + (2 * D + o * CH), WOUT_UNIT)])
            with t.loop(sp, NF, PER_IN) as i:
                load_pair(i * CH, None)
            load_ffn_out(1)
            sp.wait_ge(ada_used, t.value("folded"))
            sp.dma_start(fgain, final_gain.rearrange("(a n) -> a n", a=1).to_broadcast([P, D])).then_inc(fgain_loaded, 16)
            for tb in range(TB):
                sp.wait_ge(y_ready, tb + 1)
                sp.dma_start(out[0, tb * P:(tb + 1) * P, :], xs[:, tb]).then_inc(stored, 16)
            sp.wait_ge(stored, 16 * TB)

        N_CONSTS = 4 + PAD + 1
        N_HGRN_CONSTS = 4 + 2 * len(LEVELS)

        @block.gpsimd
        def _(pool):
            pool.memset(ident[:, :], 0.0).then_inc(consts, 1)
            pool.memset(ones[:, :], 1.0).then_inc(consts, 1)
            pool.memset(zero[:, :], 0.0).then_inc(consts, 1)
            pool.memset(padded[:, :, 0:PAD], 0.0).then_inc(consts, 1)
            for n in range(PAD):
                pool.memset(inv[:, n:n + 1], 1.0 / (n + 1)).then_inc(consts, 1)
            pool.wait_ge(consts, 4 + PAD)
            pool.affine_select(out=ident[:, :], in_=ident[:, :], compare_op=ALU.not_equal, fill=1.0,
                               base=0, pattern=[[-1, P]], channel_multiplier=1).then_inc(consts, 1)
            pool.wait_ge(w_used, HG * NCH + FFN_STEPS)
            pool.memset(keep[:, :], 1.0).then_inc(hgrn_consts, 1)
            pool.memset(masks[:, :, :], 1.0).then_inc(hgrn_consts, 1)
            pool.memset(kdec[:, :, :, :], 0.0).then_inc(hgrn_consts, 1)
            pool.wait_ge(hgrn_consts, 3)
            pool.memset(keep[:, :].rearrange("p (n c) -> p n c", c=P)[:, :, 0:1], 0.0).then_inc(hgrn_consts, 1)
            for j, h in enumerate(LEVELS):
                m = masks[:, j, :].rearrange("p (b o) -> p b o", o=h)
                pool.affine_select(out=m, in_=m, compare_op=ALU.is_ge, fill=0.0, base=0,
                                   pattern=[[-2 * h, P // (2 * h)], [0, h]], channel_multiplier=1).then_inc(hgrn_consts, 1)
            pool.wait_ge(hgrn_consts, 4 + len(LEVELS))
            for j, h in enumerate(LEVELS):
                m = masks[:, j, :].rearrange("p (b o) -> p b o", o=h)
                pool.affine_select(out=m, in_=m, compare_op=ALU.is_ge, fill=0.0, base=h - 1,
                                   pattern=[[2 * h, P // (2 * h)], [0, h]], channel_multiplier=-1).then_inc(hgrn_consts, 1)

        @block.tensor
        def _(pe):
            t = Tally()

            def bank(n):
                if t.some(f"small{n}"):
                    pe.wait_ge(small_free[n], t.value(f"small{n}"))

            def filled(ins, n):
                ins.then_inc(small_full[n], 1)
                t.tick(f"small{n}")

            def product(hi, lo, blocks, after=None, deep=False, before=None):
                par = t.get("prod") % 2
                if t.some("prod", 2):
                    pe.wait_ge(prod_free[par], t.value("prod", 0, 1, 2))
                for k in range(blocks):
                    if before is not None:
                        before(k)
                    wh, wl = split_slot(t, deep)
                    pe.wait_ge(lo_ready, t.value("step", 1))
                    for tb in range(TB):
                        ts = slice(tb * P, (tb + 1) * P)
                        o = prod[par][:, tb]
                        pe.matmul(o, hi(k)[:, ts], wh, start=(k == 0), stop=False)
                        pe.matmul(o, hi(k)[:, ts], wl, start=False, stop=False)
                        mm = pe.matmul(o, lo(k)[:, ts], wh, start=False, stop=(k == blocks - 1))
                    mm.then_inc(w_used, 1)
                    t.tick("step")
                    if after is not None:
                        after(k)
                t.tick("prod")

            def h_product(after=None, deep=False, before=None):
                product(lambda k: h_hi[:, k], lambda k: h_lo[:, k], KD, after, deep, before)

            def multiply_loads(loads):
                pe.wait_ge(unit_taken, t.value("unit"))
                for k in range(2 * loads):
                    slot = t.get("ada") % ADA
                    if k % 2 == 0:
                        pe.wait_ge(ada_loaded[slot], t.value("ada", 1, 16, ADA))
                    mm = pe.matmul(modp[:, :], cond_rows[:, k], ada[:, slot, k % 2], start=(k == 0), stop=False)
                    if k % 2:
                        mm.then_inc(pe_used, 1)
                        t.tick("ada")
                t.tick("ada", KU - loads)

            def reduce_unit(rowwise, begun=False):
                a, parts = accs[unit_buffer(t)], unit_parts(t)
                pe.wait_ge(unit_summed, t.value("unit", 1))
                if t.some("unit") and not begun:
                    pe.wait_ge(unit_taken, t.value("unit"))
                if rowwise:
                    for par in range(parts):
                        mm = pe.matmul(modp[:, :], ones[:, :], a[:, par], start=(par == 0 and not begun), stop=(par == parts - 1))
                else:
                    for j in range(HG):
                        for par in range(parts):
                            mm = pe.matmul(modp[:, j:j + 1], a[:, par, j * P:(j + 1) * P], ones[:, 0:1],
                                           start=(par == 0), stop=(par == parts - 1))
                mm.then_inc(unit_reduced, 1)
                t.tick("unit")

            def turn(block_of):
                for half in range(2):
                    bank(half)
                    for j in range(2):
                        for tb in range(TB):
                            o = (j * TB + tb) * P
                            mm = pe.transpose(small[half][:, o:o + P], block_of(tb, 2 * half + j), ident[:, :])
                    filled(mm, half)

            def turn_tok():
                turn(lambda tb, b: tok[:, tb, b * P:(b + 1) * P])

            def turn_normalised():
                t.tick("tok")
                pe.wait_ge(tok_ready, t.value("tok"))
                turn_tok()

            def features(k):
                if k == 0:
                    turn_normalised()
                if k % HG == 0 and k // HG + 1 < NCH:
                    turn_normalised()
                if k % 2 == 0:
                    t.tick("h")
                    pe.wait_ge(h_ready, t.value("h"))

            pe.wait_ge(consts, N_CONSTS)
            pe.wait_ge(params_loaded, 16 * 5)
            filled(pe.transpose(small[0][:, 0:P], rows[:, :], ident[:, :]), 0)
            reduce_unit(False)
            reduce_unit(False)
            with t.loop(pe, NCH - 1, PER_2UNITS):
                reduce_unit(False)
                reduce_unit(False)
            t.tick("ada", KU * t.get("unit"))
            turn_normalised()
            pe.wait_ge(rows_ready, 1)
            for n in range(NCH):
                multiply_loads(PE_LOADS[n])
                t.tick("h", 2)
                pe.wait_ge(h_ready, t.value("h"))
                product(lambda k: h_hi[:, n * HG + k], lambda k: h_lo[:, n * HG + k], HG)
                if n + 1 < NCH:
                    turn_normalised()
                reduce_unit(True, True)
            with t.loop(pe, NCH, PER_2UNITS):
                reduce_unit(False)
                reduce_unit(False)

            def turn_hidden():
                pe.wait_ge(prod_free[1], t.value("prod", 0, 1, 2))
                turn_tok()

            def ffn_pair(first, units):
                def in_gate(k):
                    if k == TURN and not first:
                        turn_hidden()
                    if k in [last + SUM for _, last in units]:
                        reduce_unit(False)

                def in_value(k):
                    if k + KD in [last + SUM for _, last in units]:
                        reduce_unit(False)

                h_product(in_gate, False, features if first else None)
                h_product(in_value)

            def ffn_out(layer):
                spans = OUT_UNITS[2 - layer]

                def in_out(k):
                    if k == spans[0][1] + SUM:
                        reduce_unit(True)
                    if layer == 0 and k == spans[1][1] + SUM:
                        reduce_unit(False)

                def last_hidden(k):
                    if k == KF - HG:
                        pe.wait_ge(small_free[0], t.value("small0"))
                        pe.wait_ge(small_free[1], t.value("small1"))

                with t.loop(pe, NCH // 2, PER_OUT[2 - layer]):
                    for o in range(2):
                        product(lambda k: g_hi[:, k], lambda k: g_lo[:, k], KF, in_out, False, last_hidden)

            ffn_pair(True, [])
            with t.loop(pe, 2 * NCH + 1, PER_IN_UNIT):
                ffn_pair(False, [IN_UNIT])
            with t.loop(pe, NF - 2 * NCH - 2, PER_IN):
                ffn_pair(False, [])
            turn_hidden()
            ffn_out(0)

            def self_scores(k):
                bank(k)
                pe.wait_ge(b_ready, t.value("group", 1))
                if k == 0:
                    pe.wait_ge(small_free[1], t.value("small1"))
                for hd in (2 * k, 2 * k + 1):
                    for blk in range(TB):
                        o = ((hd % 2) * TB + blk) * P
                        ts = slice(blk * P, (blk + 1) * P)
                        mm = pe.matmul(small[k][:, o:o + P], kT[:, hd, ts], qT[:, hd, ts], start=True, stop=True)
                filled(mm, k)

            def level_scores(j):
                b, H = j % 2, P // 2
                bank(b)
                t.tick("level")
                pe.wait_ge(qk_ready, t.value("level"))
                for hd in range(HG):
                    if j == 0:
                        mm = pe.matmul(small[b][:, hd * P:(hd + 1) * P], kdec[:, b, hd, 0:P], qdec[:, b, hd, :],
                                       start=True, stop=True)
                        continue
                    for blk in range(TB):
                        o = (hd * TB + blk) * H
                        mm = pe.matmul(small[b][:, o:o + H], kdec[:, b, hd, blk * P:(blk + 1) * P],
                                       qdec[:, b, hd, blk * H:(blk + 1) * H], start=True, stop=True)
                filled(mm, b)

            def turn_forget(k):
                if k == TURN + 2:
                    pe.wait_ge(prod_free[0], t.value("prod", 1, 1, 2))
                    turn_tok()

            def output():
                t.tick("group")
                pe.wait_ge(s_ready, t.value("group"))
                pe.wait_ge(prod_free[0], t.value("prod", 0, 1, 2))
                for tb in range(TB):
                    bank(tb)
                    for hd in range(HG):
                        hs = slice(hd * P, (hd + 1) * P)
                        if tb:
                            pe.matmul(small[tb][:, hs], scross[:, hd], vt[:, 0, hs], start=True, stop=False)
                        mm = pe.matmul(small[tb][:, hs], sdiag[:, hd, tb], vt[:, tb, hs], start=(tb == 0), stop=True)
                    filled(mm, tb)

            def group_work(k, every):
                if k == TURN:
                    pe.wait_ge(prod_free[1], t.value("prod", 0, 1, 2))
                    turn_tok()
                if k in (TURN + 2, TURN + 3):
                    self_scores(k - TURN - 2)
                for j in range(NL - 2):
                    if k == LEVEL_AT + every * j + (2 if every == EVERY else 3):
                        level_scores(j)
                if k == O_AT:
                    output()
                if k == HGRN_UNIT[1] + SUM:
                    reduce_unit(False)
                turn_forget(k - 3 * KD)

            assert t.get("step") % (2 * SPL) == 0
            h_product(None, True, features)
            h_product(turn_forget, True)
            with t.loop(pe, NCH - 1, PER_HGRN):
                for part in range(4):
                    h_product(lambda k: group_work(part * KD + k, EVERY), True)
            h_product(lambda k: group_work(k, EVERY_LAST), True)
            h_product(lambda k: group_work(KD + k, EVERY_LAST), True)
            for k in range(2 * KD, LEVEL_AT + EVERY_LAST * (NL - 3) + 3 + 1):
                group_work(k, EVERY_LAST)

            def turn_output(n):
                pe.wait_ge(og_ready, n + 1)
                turn(lambda tb, b: og[:, tb, (n * HG + b) * P:(n * HG + b + 1) * P])

            def output_features(k):
                if k == 0:
                    turn_output(0)
                if k % HG == 0 and k // HG + 1 < NCH - 1:
                    turn_output(k // HG + 1)
                if k == (NCH - 3) * HG:
                    output()
                if k == (NCH - 1) * HG:
                    turn_output(NCH - 1)
                if k % 2 == 0:
                    t.tick("h")
                    pe.wait_ge(h_ready, t.value("h"))

            for n in range(NCH):
                def in_wout(k):
                    if n and k == SUM:
                        reduce_unit(True)
                h_product(in_wout, False, None if n else output_features)
            reduce_unit(True)
            ffn_pair(True, [])
            with t.loop(pe, NF - 1, PER_IN):
                ffn_pair(False, [])
            turn_hidden()
            ffn_out(1)

        @block.scalar
        def _(act):
            t = Tally()

            def hi(deep=False):
                r = t.get("step") // 2 % RAW
                if t.get("step") % 2 == 0:
                    act.wait_ge(raw_loaded[r], t.value("step", 1, 16, 2 * RAW))
                if t.some("step", SPL):
                    act.wait_ge(w_used, t.value("step", 1 - (2 * SPL if deep else SPL)))
                act.activation(split_slot(t, deep)[0], raw[:, r, t.get("step") % 2], ACT.Copy).then_inc(hi_ready, 1)
                t.tick("step")

            def ahead():
                for k in range(AHEAD):
                    hi()

            def chunk(n, before=None, deep=False, done=0):
                for k in range(n):
                    if before is not None:
                        before(k)
                    if k >= done:
                        hi(deep)
                t.tick("used", n)

            def take_columns(dst):
                act.wait_ge(unit_reduced, t.value("unit", 1))
                act.activation(dst, modp[:, 0:HG], ACT.Copy).then_inc(unit_taken, 1)
                t.tick("unit")

            def take_gate():
                act.wait_ge(unit_reduced, t.value("unit", 1))
                if t.some("upd"):
                    act.wait_ge(x_updated, t.value("upd"))
                act.activation(gate[:, :], modp[:, :], ACT.Copy).then_inc(unit_taken, 1)
                t.tick("unit")

            def square(at):
                for tb in range(TB):
                    if t.some("sq"):
                        act.wait_ge(squared, t.value("sq"))
                    act.activation(junk[:, :], xs[:, tb, bass.ds(at * CH, CH)], ACT.Square,
                                   accum_out=ssq[:, tb, bass.ds(at, 1)]).then_inc(squared, 1)
                    t.tick("sq")

            def square_updated(at):
                t.tick("upd")
                act.wait_ge(x_updated, t.value("upd"))
                square(at)

            def sqrt_table():
                if t.get("table"):
                    act.wait_ge(table_ready, t.value("table"))
                act.activation(spare[:, :], zero[:, 0:1], ACT.Sqrt).then_inc(table_ready, 1)
                t.tick("table")

            def root():
                t.tick("norm")
                act.wait_ge(var_ready, t.value("norm"))
                act.activation(rstd[:, :], rstd[:, :], ACT.Sqrt).then_inc(rstd_ready, 1)

            def filled(half):
                t.tick(f"small{half}")
                act.wait_ge(small_full[half], t.value(f"small{half}"))

            def modulate(gains, shifts, n, into=None):
                for half in range(2):
                    filled(half)
                    if into is None:
                        act.wait_ge(h_ready, t.value("h", -1))
                    for j in range(2):
                        k = n * HG + 2 * half + j
                        dst = feat[:, half, j] if into is None else into[:, 2 * half + j, PAD:]
                        ins = act.activation(dst, small[half][:, j * S:(j + 1) * S], ACT.Identity,
                                             bias=shifts[:, k:k + 1], scale=gains[:, k:k + 1])
                    ins.then_inc(small_free[half], 1)
                    t.tick("h")

            def features(k, gains, shifts):
                if k == 0:
                    modulate(gains, shifts, 0)
                    modulate(gains, shifts, 1)
                if k % HG == 0 and k // HG >= 2:
                    modulate(gains, shifts, k // HG)

            def take(par, dst, func):
                act.wait_ge(w_used, t.value("used"))
                act.activation(dst[:, :, :], prod[par][:, :, :], func).then_inc(prod_free[par], 1)

            act.wait_ge(cols_ready, 1)
            act.activation(cond[:, :], cols[:, 0:KD], ACT.Silu).then_inc(cond_ready, 1)
            act.wait_ge(lb_max, 3)
            act.activation(lbt[:, 2:4], lbt[:, 2:4], ACT.Exp).then_inc(lb_exp, 1)
            act.wait_ge(consts, N_CONSTS)
            act.wait_ge(cond_ready, 1)
            for k in range(2 * max(PE_LOADS)):
                rows_k = act.activation(cond_rows[:, k], ones[:, :], ACT.Identity, bias=zero[:, 0:1], scale=cond[:, k:k + 1])
            rows_k.then_inc(rows_ready, 1)
            t.tick("small0")
            take_columns(mod[:, 0, 0:HG])
            take_columns(mod[:, 0, HG:2 * HG])
            act.wait_ge(x_loaded, 16 * TB)
            for n in range(NCH):
                square(n)
            with t.loop(act, NCH - 1, PER_2UNITS) as i:
                take_columns(mod[:, 0, bass.ds(i * 2 * HG + 2 * HG, HG)])
                take_columns(mod[:, 0, bass.ds(i * 2 * HG + 3 * HG, HG)])
            root()
            modulate(gain, mod[:, 0, 0:KD], 0, padded)
            chunk(HG)
            for n in range(NCH):
                if n:
                    square_updated(n - 1)
                if n + 1 < NCH:
                    chunk(HG)
                    act.wait_ge(h_ready, 2 * (n + 1))
                    modulate(gain, mod[:, 0, 0:KD], n + 1, padded)
                take_gate()
            take_columns(mod[:, 1, 0:HG])
            square_updated(NCH - 1)
            take_columns(mod[:, 1, HG:2 * HG])
            with t.loop(act, NCH - 1, PER_2UNITS) as i:
                take_columns(mod[:, 1, bass.ds(i * 2 * HG + 2 * HG, HG)])
                take_columns(mod[:, 1, bass.ds(i * 2 * HG + 3 * HG, HG)])

            def take_hidden(at, half):
                filled(half)
                act.activation(g_hi[:, bass.ds(at + 2 * half, 2), :],
                               small[half][:, :].rearrange("p (a s) -> p a s", a=2), ACT.Copy).then_inc(ghi_ready, 1)

            def ffn_pair(at, first, units):
                def in_gate(k):
                    if first:
                        features(k, gain, mod[:, 1, 0:KD])
                    if k == TURN + 3 and not first:
                        take_hidden(at, 0)
                    if k == TURN + 4 and not first:
                        take_hidden(at, 1)

                def in_value(k):
                    if k == EVAC:
                        take(0, tok, ACT.Silu)

                chunk(KD, in_gate, False, AHEAD if first else 0)
                chunk(KD, in_value)
                if units:
                    take_columns(units[0])

            def ffn_out(layer):
                spans = OUT_UNITS[2 - layer]
                def pair(i, end):
                    for o in range(2):
                        def in_out(k):
                            if k == EVAC + 6 and o == 1:
                                square_updated(i * 2)
                            if k == spans[0][1] + SUM + 4:
                                take_gate()
                            if layer == 0 and k == spans[1][1] + SUM + 4:
                                take_columns(mod[:, 1, bass.ds(i * 2 * HG + o * HG, HG)])
                        chunk(KF, in_out, False, AHEAD if o == 0 else 0)
                    if not end:
                        ahead()
                    sqrt_table()
                    square_updated(i * 2 + 1)

                with t.loop(act, NCH // 2 - 1, dict(PER_OUT[2 - layer], used=2 * KF, table=1)) as i:
                    pair(i, False)
                pair(NCH // 2 - 1, layer == 1)

            ahead()
            sqrt_table()
            root()
            ffn_pair(0, True, [])
            with t.loop(act, 2 * NCH, dict(PER_IN_UNIT, used=2 * KD)) as i:
                ffn_pair(i * HG, False, [mod[:, 0, bass.ds(i * HG, HG)]])
            ffn_pair(2 * NCH * HG, False, [mod[:, 1, KD:KD + HG]])
            with t.loop(act, NF - 2 * NCH - 2, dict(PER_IN, used=2 * KD)) as i:
                ffn_pair(i * HG + (2 * NCH + 1) * HG, False, [])
            ahead()
            take_hidden((NF - 1) * HG, 0)
            take_hidden((NF - 1) * HG, 1)
            ffn_out(0)

            root()

            def features_of(dst, func):
                for half in range(2):
                    filled(half)
                    act.activation(dst[:, 2 * half:2 * half + 2, :],
                                   small[half][:, :].rearrange("p (a s) -> p a s", a=2), func).then_inc(small_free[half], 1)

            def decay(j):
                t.tick("level")
                act.wait_ge(arg_ready, t.value("level"))
                act.activation(dec[:, j % 2], dec[:, j % 2], ACT.Exp).then_inc(dec_ready, 1)

            def log_forget(k):
                if k == EVAC:
                    take(0, tok, ACT.Copy)
                if k == TURN + 4:
                    features_of(fT, ACT.Sigmoid)
                if k == TURN + 7:
                    t.tick("forget")
                    act.wait_ge(f_ready, t.value("forget"))
                    act.activation(dec[:, 1], dec[:, 0], ACT.Ln).then_inc(log_ready, 1)

            def output_squares():
                for tb in range(TB):
                    filled(tb)
                    act.activation(sq[:, tb], small[tb][:, :], ACT.Square).then_inc(osq_ready, 1)

            def output_root():
                t.tick("group")
                act.wait_ge(ovar_ready, t.value("group"))
                act.activation(hn[:, :, :], hn[:, :, :], ACT.Sqrt).then_inc(orstd_ready, 1)

            def group_work(k, every, i=None):
                if k == EVAC:
                    take(1, tok, ACT.Copy)
                if k == TURN + 2:
                    features_of(qT, ACT.Copy)
                if k == KD + EVAC:
                    take(0, vt, ACT.Copy)
                if k == 2 * KD + EVAC:
                    take(1, sg, ACT.Silu)
                for j in range(NL - 2):
                    if k == LEVEL_AT + every * j + 1:
                        decay(j)
                if k == O_AT + 2:
                    t.tick("small0", NL // 2)
                    t.tick("small1", NL // 2)
                    output_squares()
                if k == O_AT + 5:
                    output_root()
                if k == 4 * KD - 1:
                    take_columns(mod[:, 1, bass.ds(i * HG + (KD + HG), HG)])
                log_forget(k - 3 * KD)

            chunk(KD, lambda k: features(k, gain, mod[:, 0, 0:KD]), True, AHEAD)
            chunk(KD, log_forget, True)
            with t.loop(act, NCH - 1, dict(PER_HGRN, used=4 * KD)) as i:
                for part in range(4):
                    chunk(KD, lambda k: group_work(part * KD + k, EVERY, i), True)
            chunk(KD, lambda k: group_work(k, EVERY_LAST), True)
            chunk(KD, lambda k: group_work(KD + k, EVERY_LAST), True)
            for k in range(2 * KD, LEVEL_AT + EVERY_LAST * (NL - 3) + 2):
                for j in range(NL - 2):
                    if k == LEVEL_AT + EVERY_LAST * j + 1:
                        decay(j)
            ahead()
            take(1, sg, ACT.Silu)
            t.tick("small0", NL // 2)
            t.tick("small1", NL // 2)

            def output_features(k):
                if k == 0:
                    modulate(cols[:, C_HGAIN:C_HGAIN + KD], zero, 0)
                    modulate(cols[:, C_HGAIN:C_HGAIN + KD], zero, 1)
                if k % HG == 0 and 2 <= k // HG < NCH - 1:
                    modulate(cols[:, C_HGAIN:C_HGAIN + KD], zero, k // HG)
                if k == (NCH - 2) * HG:
                    output_squares()
                if k == (NCH - 2) * HG + 1:
                    output_root()
                if k == KD - 2:
                    modulate(cols[:, C_HGAIN:C_HGAIN + KD], zero, NCH - 1)

            for n in range(NCH):
                def in_wout(k):
                    if n == 0:
                        output_features(k)
                    if n and k == SUM + 4:
                        take_gate()
                    if n and k == SUM + 11:
                        square_updated(n - 1)
                chunk(KD, in_wout, False, 0 if n else AHEAD)
            ahead()
            take_gate()
            sqrt_table()
            square_updated(NCH - 1)
            root()
            ffn_pair(0, True, [])
            with t.loop(act, NF - 1, dict(PER_IN, used=2 * KD)) as i:
                ffn_pair(i * HG, False, [])
            ahead()
            take_hidden((NF - 1) * HG, 0)
            take_hidden((NF - 1) * HG, 1)
            ffn_out(1)
            root()

        @block.vector
        def _(dve):
            t = Tally()

            def lo(deep=False):
                r = t.get("step") // 2 % RAW
                wh, wl = split_slot(t, deep)
                dve.wait_ge(hi_ready, t.value("step", 1))
                dve.tensor_tensor(wl, raw[:, r, t.get("step") % 2], wh, ALU.subtract).then_inc(lo_ready, 1)
                t.tick("step")

            def ahead():
                for k in range(AHEAD):
                    lo()

            def chunk(n, after=None, deep=False, done=0, before=None):
                for k in range(n):
                    if before is not None:
                        before(k)
                    if k >= done:
                        lo(deep)
                    if after is not None:
                        after(k)
                t.tick("used", n)

            def fold(k, first=0):
                slot, buf, parts = t.get("ada") % ADA, unit_buffer(t), unit_parts(t)
                w, a = ada[:, slot, k % 2], accs[buf][:, k % parts]
                if k == first and t.some("unit", 2):
                    dve.wait_ge(unit_reduced, t.value("unit", -unit_lag(t)))
                if k % 2 == 0:
                    dve.wait_ge(ada_loaded[slot], t.value("ada", 1, 16, ADA))
                if k - first < parts:
                    ins = dve.tensor_scalar(a, w, cond[:, k:k + 1], None, ALU.mult)
                else:
                    if k % 2 == parts % 2:
                        dve.wait_ge(ada_half, t.value("folded", k % 2))
                    else:
                        dve.wait_ge(ada_used, t.value("folded"))
                    ins = dve.scalar_tensor_tensor(a, w, cond[:, k:k + 1], a, ALU.mult, ALU.add)
                ins.then_inc(ada_used if k % 2 else ada_half, 1)
                if k % 2:
                    t.tick("ada")
                    t.tick("folded")
                if k == KD - 1:
                    dve.wait_ge(ada_half, t.value("folded"))
                    if parts == 1:
                        dve.wait_ge(ada_used, t.value("folded"))
                    dve.wait_ge(bias_loaded, t.value("unit", 1, 16))
                    a = accs[buf][0:1, 0]
                    dve.tensor_tensor(a, a, bias[:, :], ALU.add).then_inc(unit_summed, 1)
                    t.tick("unit")

            def unit():
                for k in range(KD):
                    fold(k)

            def norm_prepare(gains, branch):
                if gains is not None:
                    dve.wait_ge(unit_taken, t.value("unit"))
                    dve.scalar_tensor_tensor(gain[:, :], mod[:, branch, KD:2 * KD], 1.0, cols[:, gains:gains + KD],
                                             ALU.add, ALU.mult)
                dve.wait_ge(squared, t.value("sq"))
                dve.tensor_reduce(rstd[:, :], ssq[:, :, :], AXX, ALU.add).then_inc(var_step, 1)
                t.tick("var")
                dve.wait_ge(var_step, t.value("var"))
                dve.tensor_scalar(rstd[:, :], rstd[:, :], 1.0 / D, EPS, ALU.mult, ALU.add).then_inc(var_step, 1)
                t.tick("var")
                dve.wait_ge(var_step, t.value("var"))
                dve.reciprocal(rstd[:, :], rstd[:, :]).then_inc(var_ready, 1)
                t.tick("norm")
                dve.wait_ge(rstd_ready, t.value("norm"))

            def normalise(n):
                if t.some("small1"):
                    dve.wait_ge(small_full[1], t.value("small1"))
                if t.some("upd"):
                    dve.wait_ge(x_updated, t.value("upd"))
                for tb in range(TB):
                    ins = dve.tensor_scalar(tok[:, tb], xs[:, tb, n * CH:(n + 1) * CH], rstd[:, tb:tb + 1], None, ALU.mult)
                ins.then_inc(tok_ready, 1)

            def split_h(src, k, n):
                dve.tensor_copy(h_hi[:, k:k + n], src).then_inc(h_high, 1)
                t.tick("hh")
                dve.wait_ge(h_high, t.value("hh"))
                return dve.tensor_tensor(h_lo[:, k:k + n], src, h_hi[:, k:k + n], ALU.subtract)

            def split_feat(n):
                for half in range(2):
                    t.tick(f"small{half}")
                    dve.wait_ge(small_free[half], t.value(f"small{half}"))
                    split_h(feat[:, half], n * HG + 2 * half, 2).then_inc(h_ready, 1)

            def normalise_ahead(n):
                t.n["small1"] += 1
                normalise(n)
                t.n["small1"] -= 1

            def features(k):
                if k == 0:
                    normalise(0)
                    for n in range(2):
                        normalise_ahead(n + 1)
                        split_feat(n)
                if k % HG == 0 and k // HG >= 2:
                    if k // HG + 1 < NCH:
                        normalise_ahead(k // HG + 1)
                    split_feat(k // HG)

            def update(par, at, gates=gate[:, :], later=0):
                dve.wait_ge(w_used, t.value("used"))
                dve.wait_ge(unit_taken, t.value("unit", -later))
                if t.some("upd"):
                    dve.wait_ge(x_updated, t.value("upd"))
                t.tick("upd")
                term = gates.unsqueeze(1).to_broadcast([P, TB, CH])
                dve.tensor_tensor(tok[:, :, :], prod[par][:, :, :], term, ALU.mult).then_inc(prod_free[par], 1)
                dve.wait_ge(prod_free[par], t.value("prod", 1, 1, 2))
                xc = xs[:, :, bass.ds(at * CH, CH)]
                dve.tensor_tensor(xc, xc, tok[:, :, :], ALU.add).then_inc(x_updated, 1)

            dve.wait_ge(small_full[0], 1)
            dve.tensor_copy(cols[:, :], small[0][:, 0:P]).then_inc(small_free[0], 1)
            t.tick("small0")
            dve.wait_ge(small_free[0], 1)
            lb = cols[:, C_LB:C_LB + 2 * KD].rearrange("p (l k) -> p l k", l=2)
            dve.tensor_copy(lbt[:, 2:4], lb).then_inc(cols_ready, 1)
            dve.tensor_tensor(lbt[:, 0], lb[:, 0], lb[:, 1], ALU.max).then_inc(lb_max, 1)
            dve.wait_ge(lb_max, 1)
            dve.wait_ge(cols_ready, 1)
            for l in range(2):
                dve.tensor_tensor(lbt[:, 2 + l], lbt[:, 2 + l], lbt[:, 0], ALU.subtract).then_inc(lb_max, 1)
            dve.wait_ge(lb_exp, 1)
            dve.tensor_tensor(lbt[:, 0], lbt[:, 2], lbt[:, 3], ALU.add).then_inc(lb_ready, 1)
            dve.wait_ge(lb_ready, 1)
            dve.reciprocal(lbt[:, 1], lbt[:, 0]).then_inc(lb_ready, 1)
            dve.wait_ge(lb_ready, 2)
            for l in range(2):
                dve.tensor_tensor(lbt[:, 2 + l], lbt[:, 2 + l], lbt[:, 1], ALU.mult).then_inc(lb_ready, 1)
            dve.wait_ge(lb_ready, 4)
            dve.tensor_tensor(lbt[:, 0], lbt[:, 2], lbt[:, 3], ALU.add).then_inc(lb_ready, 1)
            dve.wait_ge(lb_ready, 5)
            dve.tensor_tensor(lower[:, :], lbt[:, 0], lbt[:, 2], ALU.subtract).then_inc(lb_ready, 1)
            dve.wait_ge(lb_ready, 6)
            dve.tensor_scalar(upper[:, :], lower[:, :], -1.0, 1.0, ALU.mult, ALU.add).then_inc(lb_ready, 1)
            dve.wait_ge(cond_ready, 1)
            t.tick("sq", NCH * TB)
            unit()
            unit()
            with t.loop(dve, NCH - 1, PER_2UNITS):
                unit()
                unit()

            def pool_group(n, w):
                src, span, lo_end = padded, 1, 1
                step = [t.get("pool")]

                def done(ins):
                    ins.then_inc(pool_step, 1)
                    t.tick("pool")
                    dve.wait_ge(pool_step, t.value("pool"))

                while span < w:
                    dst = win[0] if src is not win[0] else win[1]
                    done(dve.tensor_tensor(dst[:, :, lo_end:], src[:, :, lo_end:],
                                           src[:, :, lo_end - span:PAD + S - span], ALU.add))
                    src, span = dst, 2 * span
                    lo_end += span
                h = padded[:, :, PAD:]
                done(dve.scalar_tensor_tensor(diff[:, :, :], src[:, :, PAD:], 1.0 / w, h, ALU.mult, ALU.subtract))
                done(dve.tensor_tensor(edge[:, :, 0:w], src[:, :, PAD:PAD + w],
                                       inv[:, 0:w].unsqueeze(1).to_broadcast([P, HG, w]), ALU.mult))
                done(dve.tensor_tensor(diff[:, :, 0:w], edge[:, :, 0:w], h[:, :, 0:w], ALU.subtract))
                split_h(diff[:, :, :], n * HG, HG).then_inc(h_ready, 2)

            norm_prepare(C_GMIX, 0)
            def pool_update(n):
                dve.wait_ge(pscale_loaded, 16)
                dve.wait_ge(unit_taken, 2 * NCH + n + 1)
                dve.tensor_tensor(pscale[:, n], pscale[:, n], gate[:, :], ALU.mult).then_inc(pscale_ready, 1)
                dve.wait_ge(pscale_ready, n + 1)
                dve.wait_ge(small_full[1], t.value("small1"))
                update(n % 2, n, pscale[:, n], t.get("unit") - (2 * NCH + n + 1))
                t.tick("prod")
                t.tick("sq", TB)

            dve.wait_ge(consts, N_CONSTS)
            normalise(0)
            for n, w in enumerate(WINDOWS):
                for k in range(HG):
                    lo()
                t.tick("small0")
                t.tick("small1")
                dve.wait_ge(small_free[0], t.value("small0"))
                dve.wait_ge(small_free[1], t.value("small1"))
                pool_group(n, w)
                if n:
                    pool_update(n - 1)
                t.tick("used", HG)
                if n + 1 < NCH:
                    normalise(n + 1)
                t.tick("ada", PE_LOADS[n])
                for k in range(2 * PE_LOADS[n], KD):
                    fold(k, 2 * PE_LOADS[n])
            unit()
            pool_update(NCH - 1)
            unit()
            with t.loop(dve, NCH - 1, PER_2UNITS):
                unit()
                unit()

            def take_value():
                dve.wait_ge(w_used, t.value("used"))
                dve.wait_ge(prod_free[0], t.value("prod", 0, 1, 2))
                dve.tensor_tensor(tok[:, :, :], tok[:, :, :], prod[1][:, :, :], ALU.mult).then_inc(prod_free[1], 1)

            def low_hidden(at, half):
                t.tick(f"small{half}")
                t.tick("hid")
                dve.wait_ge(ghi_ready, t.value("hid"))
                blocks = bass.ds(at + 2 * half, 2)
                dve.tensor_tensor(g_lo[:, blocks, :], small[half][:, :].rearrange("p (a s) -> p a s", a=2),
                                  g_hi[:, blocks, :], ALU.subtract).then_inc(small_free[half], 1)

            def ffn_pair(at, first, units):
                def in_gate(k):
                    if k == EVAC - 1 and not first:
                        take_value()
                    for span in units:
                        for b in due(k, KD, *span):
                            fold(b)
                    if k == TURN + 3 and not first:
                        low_hidden(at, 0)
                    if k == TURN + 4 and not first:
                        low_hidden(at, 1)

                def in_value(k):
                    for span in units:
                        for b in due(k + KD, KD, *span):
                            fold(b)

                chunk(KD, in_gate, False, AHEAD if first else 0, features if first else None)
                chunk(KD, in_value)
                t.tick("prod", 2)

            def ffn_out(layer):
                spans = OUT_UNITS[2 - layer]
                def pair(i, end):
                    for o in range(2):
                        def in_out(k):
                            if k == EVAC + 1 and o == 1:
                                update(0, i * 2, gate[:, :], len(spans) - 1)
                            for span in spans:
                                for b in due(k, KD, *span):
                                    fold(b)
                        chunk(KF, in_out, False, AHEAD if o == 0 else 0)
                    if not end:
                        ahead()
                    update(1, i * 2 + 1, gate[:, :], len(spans) - 1)
                    t.tick("prod", 2)
                    t.tick("sq", 2 * TB)

                with t.loop(dve, NCH // 2 - 1, dict(PER_OUT[2 - layer], used=2 * KF)) as i:
                    pair(i, False)
                pair(NCH // 2 - 1, layer == 1)

            ahead()
            norm_prepare(C_GFFN, 1)
            ffn_pair(0, True, [])
            with t.loop(dve, 2 * NCH, dict(PER_IN_UNIT, used=2 * KD)) as i:
                ffn_pair(i * HG, False, [IN_UNIT])
            ffn_pair(2 * NCH * HG, False, [IN_UNIT])
            with t.loop(dve, NF - 2 * NCH - 2, dict(PER_IN, used=2 * KD)) as i:
                ffn_pair(i * HG + (2 * NCH + 1) * HG, False, [])
            ahead()
            take_value()
            low_hidden((NF - 1) * HG, 0)
            low_hidden((NF - 1) * HG, 1)
            ffn_out(0)

            norm_prepare(C_GMIX + KD, 0)
            b4 = lambda a, h: a.rearrange("p a s -> p (a s)").rearrange("p (n two h) -> p n two h", two=2, h=h)

            def forget(i):
                for half in range(2):
                    t.tick(f"small{half}")
                    dve.wait_ge(small_free[half], t.value(f"small{half}"))
                for hd in range(HG):
                    ins = dve.tensor_scalar(fT[:, hd], fT[:, hd], upper[:, bass.ds(i * HG + hd, 1)],
                                            lower[:, bass.ds(i * HG + hd, 1)], ALU.mult, ALU.add)
                ins.then_inc(fT_ready, 1)
                t.tick("bs")
                dve.wait_ge(fT_ready, t.value("bs"))
                dve.tensor_scalar(kT[:, :, :], fT[:, :, :], -1.0, 1.0, ALU.mult, ALU.add)
                dve.tensor_scalar(dec[:, 0], fT[:, :, :], LN_FLOOR, None, ALU.max).then_inc(f_ready, 1)

            def cumulate():
                t.tick("logs")
                dve.wait_ge(log_ready, t.value("logs"))
                dve.tensor_tensor_scan(bT[:, :, :].rearrange("p a s -> p (a s)"), keep[:, :],
                                       dec[:, 1].rearrange("p a s -> p (a s)"), 0.0, ALU.mult, ALU.add).then_inc(b_ready, 1)

            def exponents(j):
                d = dec[:, j % 2]
                if j == 0:
                    dve.wait_ge(b_ready, t.value("group", 1))
                    ref = bT[:, :, P - 1:P].to_broadcast([P, HG, P])
                    dve.tensor_tensor(d[:, :, 0:P], ref, bT[:, :, 0:P], ALU.subtract)
                    dve.tensor_copy(d[:, :, P:], bT[:, :, P:]).then_inc(arg_ready, 1)
                    return
                h = LEVELS[j - 1]
                b, e = b4(bT[:, :, :], h), b4(d, h)
                ref = b[:, :, 0, h - 1:h].to_broadcast([P, HG * S // (2 * h), h])
                dve.tensor_tensor(e[:, :, 0], ref, b[:, :, 0], ALU.subtract)
                dve.tensor_tensor(e[:, :, 1], b[:, :, 1], ref, ALU.subtract).then_inc(arg_ready, 1)

            def decayed(j):
                t.tick("level")
                dve.wait_ge(dec_ready, t.value("level"))
                d, kd, qd = dec[:, j % 2], kdec[:, j % 2], qdec[:, j % 2]
                if j == 0:
                    dve.tensor_tensor(kd[:, :, 0:P], kT[:, :, 0:P], d[:, :, 0:P], ALU.mult)
                    dve.tensor_tensor(qd, qT[:, :, P:], d[:, :, P:], ALU.mult).then_inc(qk_ready, 1)
                    return
                h = LEVELS[j - 1]
                dve.tensor_tensor(b4(kd, h)[:, :, 0], b4(kT[:, :, :], h)[:, :, 0], b4(d, h)[:, :, 0], ALU.mult)
                dve.tensor_tensor(qd.rearrange("p a s -> p (a s)").rearrange("p (n h) -> p n h", h=h),
                                  b4(qT[:, :, :], h)[:, :, 1], b4(d, h)[:, :, 1], ALU.mult).then_inc(qk_ready, 1)

            def scores(k):
                bk = k % 2
                t.tick(f"small{bk}")
                dve.wait_ge(small_full[bk], t.value(f"small{bk}"))
                if k < 2:
                    dve.tensor_tensor(sdiag[:, 2 * k:2 * k + 2].rearrange("p a b s -> p (a b) s"),
                                      small[bk][:, :].rearrange("p (n s) -> p n s", s=P),
                                      ident[:, :].unsqueeze(1).to_broadcast([P, 2 * TB, P]), ALU.mult).then_inc(small_free[bk], 1)
                    return
                if k == 2:
                    dve.tensor_copy(scross[:, :, :].rearrange("p a s -> p (a s)"), small[bk][:, :]).then_inc(small_free[bk], 1)
                    return
                h = LEVELS[k - 3]
                m = masks[:, k - 3, :].unsqueeze(1).to_broadcast([P, HG * TB, P // 2])
                if k > 3:
                    dve.wait_ge(s_masked, t.value("sm"))
                dve.tensor_tensor(smask[:, :, :], small[bk][:, :].rearrange("p (n s) -> p n s", s=P // 2), m,
                                  ALU.mult).then_inc(small_free[bk], 1)
                dve.wait_ge(small_free[bk], t.value(f"small{bk}"))
                if k == 3:
                    dve.wait_ge(small_free[1], t.value("small1", -1))
                target = b4(sdiag[:, :, :, :].rearrange("p a b s -> p (a b) s"), h)[:, :, 1]
                dve.tensor_tensor(target, target, smask[:, :, :].rearrange("p n s -> p (n s)").rearrange("p (n h) -> p n h", h=h),
                                  ALU.add).then_inc(s_ready if k == NL - 1 else s_masked, 1)
                if k < NL - 1:
                    t.tick("sm")

            def output_norm():
                for tb in range(TB):
                    t.tick(f"small{tb}")
                t.tick("group")
                dve.wait_ge(osq_ready, t.value("group", 0, TB))
                dve.tensor_reduce(hn[:, :, :].rearrange("p a b -> p (a b)"),
                                  sq.rearrange("p a (b s) -> p (a b) s", s=P), AXX, ALU.add).then_inc(ovar_step, 1)
                t.tick("ov")
                dve.wait_ge(ovar_step, t.value("ov"))
                dve.tensor_scalar(hn[:, :, :], hn[:, :, :], 1.0 / P, EPS, ALU.mult, ALU.add).then_inc(ovar_step, 1)
                t.tick("ov")
                dve.wait_ge(ovar_step, t.value("ov"))
                dve.reciprocal(hn[:, :, :], hn[:, :, :]).then_inc(ovar_ready, 1)

            def output_gate(i):
                dve.wait_ge(orstd_ready, t.value("group"))
                for tb in range(TB):
                    o = og[:, tb, bass.ds(i * CH, CH)].rearrange("p (b s) -> p b s", s=P)
                    dve.tensor_tensor(o, small[tb][:, :].rearrange("p (b s) -> p b s", s=P),
                                      hn[:, tb].unsqueeze(2).to_broadcast([P, HG, P]), ALU.mult).then_inc(small_free[tb], 1)
                for tb in range(TB):
                    dve.wait_ge(small_free[tb], t.value(f"small{tb}"))
                dve.wait_ge(prod_free[1], t.value("prod", 1, 1, 2))
                o = og[:, :, bass.ds(i * CH, CH)]
                dve.tensor_tensor(o, o, sg[:, :, :], ALU.mult).then_inc(og_ready, 1)

            def forget_work(k, i):
                if k == TURN + 5:
                    forget(i)
                if k == KD - 1:
                    cumulate()

            def group_work(k, i, every):
                for j in range(NL - 2):
                    at = LEVEL_AT + every * j
                    if k == at:
                        exponents(j)
                    if k == at + 2:
                        decayed(j)
                if k == LEVEL_AT + 1:
                    for half in range(2):
                        t.tick(f"small{half}")
                        dve.wait_ge(small_free[half], t.value(f"small{half}"))
                if k in (LEVEL_AT + 3, LEVEL_AT + 4):
                    scores(k - LEVEL_AT - 3)
                for j in range(NL - 2):
                    if k == LEVEL_AT + every * j + (5 if every == EVERY else 6):
                        scores(2 + j)
                if k == O_AT + 3:
                    output_norm()
                if k == O_AT + 5:
                    output_gate(i)
                if every == EVERY:
                    for b in due(k, KD, *HGRN_UNIT):
                        fold(b)
                forget_work(k - 3 * KD, i + 1)

            chunk(KD, None, True, AHEAD, features)
            dve.wait_ge(hgrn_consts, N_HGRN_CONSTS)
            chunk(KD, lambda k: forget_work(k, 0), True)
            t.tick("prod", 2)
            with t.loop(dve, NCH - 1, dict(PER_HGRN, used=4 * KD, bs=1, logs=1, sm=NL - 4, ov=2)) as i:
                for part in range(4):
                    chunk(KD, lambda k: group_work(part * KD + k, i, EVERY), True)
                t.tick("prod", 4)
            chunk(KD, lambda k: group_work(k, NCH - 1, EVERY_LAST), True)
            chunk(KD, lambda k: group_work(KD + k, NCH - 1, EVERY_LAST), True)
            for k in range(2 * KD, LEVEL_AT + EVERY_LAST * (NL - 3) + 6 + 1):
                group_work(k, NCH - 1, EVERY_LAST)
            ahead()
            dve.wait_ge(w_used, t.value("used"))

            def output_features(k):
                if k == 0:
                    split_feat(0)
                    split_feat(1)
                if k % HG == 0 and 2 <= k // HG < NCH - 1:
                    split_feat(k // HG)
                if k == (NCH - 2) * HG:
                    output_norm()
                if k == (NCH - 2) * HG + 1:
                    output_gate(NCH - 1)
                    t.tick("prod", 2)
                if k == KD - 2:
                    split_feat(NCH - 1)

            for n in range(NCH):
                def in_wout(k):
                    if n and k == SUM + 5:
                        update((n - 1) % 2, n - 1)
                        t.tick("prod")
                        t.tick("sq", TB)
                    for b in due(k, KD, *WOUT_UNIT):
                        fold(b)
                chunk(KD, in_wout, False, 0 if n else AHEAD, None if n else output_features)
            ahead()
            update((NCH - 1) % 2, NCH - 1)
            t.tick("prod")
            t.tick("sq", TB)
            norm_prepare(C_GFFN + KD, 1)
            ffn_pair(0, True, [])
            with t.loop(dve, NF - 1, dict(PER_IN, used=2 * KD)) as i:
                ffn_pair(i * HG, False, [])
            ahead()
            take_value()
            low_hidden((NF - 1) * HG, 0)
            low_hidden((NF - 1) * HG, 1)
            ffn_out(1)
            norm_prepare(None, 0)
            dve.wait_ge(fgain_loaded, 16)
            for tb in range(TB):
                dve.scalar_tensor_tensor(xs[:, tb], xs[:, tb], rstd[:, tb:tb + 1], fgain, ALU.mult, ALU.mult).then_inc(y_ready, 1)


_NAMES = ["x", "c", "norm_mix_gain", "norm_ffn_gain", "w_ada", "b_ada", "pool_w", "pool_scale", "hgrn_w_in",
          "hgrn_w_out", "hgrn_norm_gain", "hgrn_lb", "w_ffn_in", "w_ffn_out", "final_gain"]


def kernel(**inputs):
    import concourse.bacc as bacc
    from concourse.bass_utils import run_bass_kernel_spmd

    nc = bacc.Bacc("TRN2", target_bir_lowering=False, num_devices=1)
    arrays, args = {}, []
    for name in _NAMES:
        a = np.ascontiguousarray(inputs[name])
        arrays[f"in_{name}"] = a
        args.append(nc.dram_tensor(f"in_{name}", a.shape, mybir.dt.from_np(a.dtype), kind="ExternalInput").ap())
    out = nc.dram_tensor("out", inputs["x"].shape, F32, kind="ExternalOutput").ap()
    build(nc, *args, out)
    result = run_bass_kernel_spmd(nc, [arrays], core_ids=[0])
    return result.results[0]["out"]
```
